# Optimizing a Trainium2 kernel written in Bass

```python
import math
import jax
import jax.numpy as jnp
from jax import lax
import numpy as np
import jax, jax.numpy as jnp

D_MODEL = 2048
BATCH = 1
SEQ = 512
DEPTH = 1

MEM_LEN = 256
MIX_W = D_MODEL
LRU_W = MIX_W // 4
LRU_BLOCKS = 4
LRU_CONV = 4
LRU_C = 8.0
ML_W = 3 * MIX_W // 8
ML_HEADS = 4
ML_DH = ML_W // ML_HEADS
ML_QKV_BLOCK = 4
ML_CONV = 4
ML_CHUNK = 128
MO_W = MIX_W - LRU_W - ML_W
MO_HEADS = 6
MO_DH = MO_W // MO_HEADS
MOBA_BLOCK = 256
MOBA_TOPK = 3
MOBA_Q_CHUNK = 16
XA_HEADS = 4
XA_DH = 128
XA_W = XA_HEADS * XA_DH

RMS_EPS = 1e-6
LN_EPS = 1e-5
NEG_INF = -1e30

SPLIT_SIZES = (LRU_W, LRU_W, ML_W, ML_W, ML_W, ML_HEADS, ML_HEADS, MO_W, MO_W, MO_W, MO_W)
IN_COLS = sum(SPLIT_SIZES)
SPLIT_POINTS = tuple(int(v) for v in np.cumsum(SPLIT_SIZES)[:-1])


def rms_norm(x, g):
    x32 = x.astype(jnp.float32)
    y = x32 * lax.rsqrt(jnp.mean(x32 * x32, axis=-1, keepdims=True) + RMS_EPS)
    return (y * g.astype(jnp.float32)).astype(x.dtype)

def causal_conv(x, w, b):
    K = w.shape[0]
    T = x.shape[1]
    xp = jnp.pad(x, ((0, 0), (K - 1, 0), (0, 0)))
    return sum(xp[:, j:j + T] * w[j] for j in range(K)) + b

def block_diag(x, w):
    G, bi, bo = w.shape
    xs = x.reshape(x.shape[:-1] + (G, bi))
    return jnp.einsum('...gi,gio->...go', xs, w).reshape(x.shape[:-1] + (G * bo,))

def alibi_slopes(n):
    def pow2(m):
        start = 2.0 ** (-8.0 / m)
        return [start ** (i + 1) for i in range(m)]
    if math.log2(n).is_integer():
        s = pow2(n)
    else:
        c = 2 ** int(math.floor(math.log2(n)))
        s = pow2(c) + pow2(2 * c)[0::2][:n - c]
    return jnp.array(s, dtype=jnp.float32)

def rg_lru_branch(xb, zb, conv_w, conv_b, wa, ba, wx, bx, lam):
    xc = causal_conv(xb, conv_w, conv_b).astype(jnp.float32)
    r = jax.nn.sigmoid(block_diag(xc, wa) + ba)
    i = jax.nn.sigmoid(block_diag(xc, wx) + bx)
    log_a = -LRU_C * r * jax.nn.softplus(-lam.astype(jnp.float32))
    a = jnp.exp(log_a)
    u = jnp.sqrt(-jnp.expm1(2.0 * log_a)) * (i * xc)

    def combine(left, right):
        a1, b1 = left
        a2, b2 = right
        return a1 * a2, a2 * b1 + b2

    _, h = lax.associative_scan(combine, (a, u), axis=1)
    return (h * jax.nn.silu(zb.astype(jnp.float32))).astype(xb.dtype)

def mlstm_chunkwise(q, k, v, ig, lf):
    B, H, T, dh = q.shape
    L = ML_CHUNK
    nc = T // L
    q, k, v = (t.reshape(B, H, nc, L, dh) for t in (q, k, v))
    ig = ig.reshape(B, H, nc, L)
    lf = lf.reshape(B, H, nc, L)
    b = jnp.cumsum(lf, axis=-1)
    g = b[..., -1]
    a = g[..., None] - b + ig
    m_loc = jnp.max(a, axis=-1)
    w = jnp.exp(a - m_loc[..., None])
    c_loc = jnp.einsum('bhcl,bhcld,bhcle->bhcde', w, k, v)
    n_loc = jnp.einsum('bhcl,bhcld->bhcd', w, k)

    def step(carry, inp):
        c_st, n_st, m_st = carry
        c_l, n_l, m_l, g_c = inp
        m_new = jnp.maximum(g_c + m_st, m_l)
        s_old = jnp.exp(g_c + m_st - m_new)
        s_new = jnp.exp(m_l - m_new)
        c_new = s_old[..., None, None] * c_st + s_new[..., None, None] * c_l
        n_new = s_old[..., None] * n_st + s_new[..., None] * n_l
        return (c_new, n_new, m_new), (c_st, n_st, m_st)

    init = (jnp.zeros((B, H, dh, dh), jnp.float32), jnp.zeros((B, H, dh), jnp.float32),
            jnp.zeros((B, H), jnp.float32))
    xs = tuple(jnp.moveaxis(t, 2, 0) for t in (c_loc, n_loc, m_loc, g))
    _, (c_prev, n_prev, m_prev) = lax.scan(step, init, xs)
    c_prev = jnp.moveaxis(c_prev, 0, 2)
    n_prev = jnp.moveaxis(n_prev, 0, 2)
    m_prev = jnp.moveaxis(m_prev, 0, 2)
    causal = jnp.tril(jnp.ones((L, L), dtype=bool))
    d = jnp.where(causal, b[..., :, None] - b[..., None, :] + ig[..., None, :], -jnp.inf)
    inter = b + m_prev[..., None]
    m = jnp.maximum(inter, jnp.max(d, axis=-1))
    s = jnp.einsum('bhcjd,bhcsd->bhcjs', q, k) * jnp.exp(d - m[..., None])
    s_int = jnp.exp(inter - m)
    num = (jnp.einsum('bhcjs,bhcsd->bhcjd', s, v)
           + s_int[..., None] * jnp.einsum('bhcjd,bhcde->bhcje', q, c_prev))
    den = jnp.sum(s, axis=-1) + s_int * jnp.einsum('bhcjd,bhcd->bhcj', q, n_prev)
    h = num / jnp.maximum(jnp.abs(den), jnp.exp(-m))[..., None]
    return h.reshape(B, H, T, dh)

def mlstm_branch(u, o, z, ig_pre, fg_pre, conv_w, conv_b, wq, wk, wv, bi, bf, norm_g):
    B, T, _ = u.shape
    uc = jax.nn.silu(causal_conv(u, conv_w, conv_b))
    q = block_diag(uc, wq)
    k = block_diag(uc, wk) * (ML_DH ** -0.5)
    v = block_diag(u, wv)

    def heads(t):
        return t.astype(jnp.float32).reshape(B, T, ML_HEADS, ML_DH).transpose(0, 2, 1, 3)

    ig = (ig_pre.astype(jnp.float32) + bi).transpose(0, 2, 1)
    lf = jax.nn.log_sigmoid(fg_pre.astype(jnp.float32) + bf).transpose(0, 2, 1)
    h = mlstm_chunkwise(heads(q), heads(k), heads(v), ig, lf).transpose(0, 2, 1, 3)
    h = jax.nn.sigmoid(o.astype(jnp.float32)).reshape(B, T, ML_HEADS, ML_DH) * h
    mu = jnp.mean(h, axis=-1, keepdims=True)
    var = jnp.mean(jnp.square(h - mu), axis=-1, keepdims=True)
    hn = (h - mu) * lax.rsqrt(var + LN_EPS) * norm_g.astype(jnp.float32).reshape(ML_HEADS, ML_DH)
    return (hn.reshape(B, T, ML_W) * jax.nn.silu(z.astype(jnp.float32))).astype(u.dtype)

def moba_attention(q, k, v):
    B, H, T, dh = q.shape
    nb = -(-T // MOBA_BLOCK)
    tp = nb * MOBA_BLOCK
    pad = ((0, 0), (0, 0), (0, tp - T), (0, 0))
    q, k, v = (jnp.pad(t, pad) for t in (q, k, v))
    kb = k.reshape(B, H, nb, MOBA_BLOCK, dh)
    vb = v.reshape(B, H, nb, MOBA_BLOCK, dh)
    kmean = jnp.mean(kb.astype(jnp.float32), axis=3)
    n_sel = min(MOBA_TOPK, nb - 1)
    slopes = alibi_slopes(H)
    scale = dh ** -0.5
    nq = tp // MOBA_Q_CHUNK
    qc = jnp.moveaxis(q.reshape(B, H, nq, MOBA_Q_CHUNK, dh), 2, 0)
    bidx = jnp.arange(B)[:, None, None, None]
    hidx = jnp.arange(H)[None, :, None, None]
    s_local = jnp.arange(MOBA_BLOCK)

    def one_chunk(args):
        qch, ci = args
        qch = qch.astype(jnp.float32)
        t = ci * MOBA_Q_CHUNK + jnp.arange(MOBA_Q_CHUNK)
        bq = (ci * MOBA_Q_CHUNK) // MOBA_BLOCK
        k_own = lax.dynamic_index_in_dim(kb, bq, axis=2, keepdims=False).astype(jnp.float32)
        v_own = lax.dynamic_index_in_dim(vb, bq, axis=2, keepdims=False).astype(jnp.float32)
        dist_own = (t[:, None] - (bq * MOBA_BLOCK + s_local)[None, :]).astype(jnp.float32)
        l_own = jnp.einsum('bhqd,bhsd->bhqs', qch, k_own) * scale - slopes[:, None, None] * dist_own
        l_own = jnp.where(dist_own >= 0, l_own, NEG_INF)
        if n_sel == 0:
            p_own = jax.nn.softmax(l_own, axis=-1)
            return jnp.einsum('bhqs,bhsd->bhqd', p_own, v_own)
        gate = jnp.einsum('bhqd,bhnd->bhqn', qch, kmean)
        gate = jnp.where(jnp.arange(nb) < bq, gate, -jnp.inf)
        _, idx = lax.top_k(gate, n_sel)
        k_sel = kb[bidx, hidx, idx].astype(jnp.float32)
        v_sel = vb[bidx, hidx, idx].astype(jnp.float32)
        dist_sel = (t[:, None, None] - (idx[..., None] * MOBA_BLOCK + s_local)).astype(jnp.float32)
        l_sel = (jnp.einsum('bhqd,bhqnsd->bhqns', qch, k_sel) * scale
                 - slopes[:, None, None, None] * dist_sel)
        l_sel = jnp.where((jnp.arange(n_sel) < bq)[:, None], l_sel, NEG_INF)
        n_past = n_sel * MOBA_BLOCK
        logits = jnp.concatenate(
            [l_sel.reshape(B, H, MOBA_Q_CHUNK, n_past), l_own], axis=-1)
        p = jax.nn.softmax(logits, axis=-1)
        p_sel = p[..., :n_past].reshape(B, H, MOBA_Q_CHUNK, n_sel, MOBA_BLOCK)
        p_own = p[..., n_past:]
        return (jnp.einsum('bhqns,bhqnsd->bhqd', p_sel, v_sel)
                + jnp.einsum('bhqs,bhsd->bhqd', p_own, v_own))

    out = lax.map(one_chunk, (qc, jnp.arange(nq)))
    out = jnp.moveaxis(out, 0, 2).reshape(B, H, tp, dh)
    return out[:, :, :T]

def moba_branch(qb, kb, vb, zb):
    B, T, _ = qb.shape

    def heads(t):
        return t.reshape(B, T, MO_HEADS, MO_DH).transpose(0, 2, 1, 3)

    o = moba_attention(heads(qb), heads(kb), heads(vb)).transpose(0, 2, 1, 3).reshape(B, T, MO_W)
    return (o * jax.nn.silu(zb.astype(jnp.float32))).astype(qb.dtype)

def memory_cross_attention(h, mem_n, wq, wkv, wo):
    B, T, _ = h.shape
    M = mem_n.shape[1]
    q = (h @ wq).reshape(B, T, XA_HEADS, XA_DH)
    k, v = jnp.split(mem_n @ wkv, 2, axis=-1)
    k = k.reshape(B, M, XA_HEADS, XA_DH)
    v = v.reshape(B, M, XA_HEADS, XA_DH)
    s = jnp.einsum('bthd,bmhd->bhtm', q, k).astype(jnp.float32) * (XA_DH ** -0.5)
    p = jax.nn.softmax(s, axis=-1).astype(v.dtype)
    o = jnp.einsum('bhtm,bmhd->bthd', p, v).reshape(B, T, XA_W)
    return o @ wo

def first_inputs(seed: int = 0) -> dict:
    key = jax.random.key(seed)
    ks = jax.random.split(key, 26)

    def nrm(k, shape, scale):
        return scale * jax.random.normal(k, shape, jnp.float32)

    def gain(k, shape):
        return 1.0 + 0.02 * jax.random.normal(k, shape, jnp.float32)

    u = jax.random.uniform(ks[10], (DEPTH, LRU_W), jnp.float32, 0.9, 0.999)
    a = u ** (1.0 / LRU_C)
    lam = jnp.log(a) - jnp.log1p(-a)
    bl = LRU_W // LRU_BLOCKS
    nqkv = ML_W // ML_QKV_BLOCK
    return {
        "x": nrm(ks[0], (BATCH, SEQ, D_MODEL), 1.0),
        "mem": nrm(ks[1], (BATCH, MEM_LEN, D_MODEL), 1.0),
        "mix_norm_g": gain(ks[2], (DEPTH, D_MODEL)),
        "w_in": nrm(ks[3], (DEPTH, D_MODEL, IN_COLS), D_MODEL ** -0.5),
        "lru_conv_w": nrm(ks[4], (DEPTH, LRU_CONV, LRU_W), LRU_CONV ** -0.5),
        "lru_conv_b": nrm(ks[5], (DEPTH, LRU_W), 0.02),
        "lru_wa": nrm(ks[6], (DEPTH, LRU_BLOCKS, bl, bl), bl ** -0.5),
        "lru_ba": nrm(ks[7], (DEPTH, LRU_W), 0.02),
        "lru_wx": nrm(ks[8], (DEPTH, LRU_BLOCKS, bl, bl), bl ** -0.5),
        "lru_bx": nrm(ks[9], (DEPTH, LRU_W), 0.02),
        "lru_lambda": lam,
        "ml_conv_w": nrm(ks[11], (DEPTH, ML_CONV, ML_W), ML_CONV ** -0.5),
        "ml_conv_b": nrm(ks[12], (DEPTH, ML_W), 0.02),
        "ml_wq": nrm(ks[13], (DEPTH, nqkv, ML_QKV_BLOCK, ML_QKV_BLOCK), ML_QKV_BLOCK ** -0.5),
        "ml_wk": nrm(ks[14], (DEPTH, nqkv, ML_QKV_BLOCK, ML_QKV_BLOCK), ML_QKV_BLOCK ** -0.5),
        "ml_wv": nrm(ks[15], (DEPTH, nqkv, ML_QKV_BLOCK, ML_QKV_BLOCK), ML_QKV_BLOCK ** -0.5),
        "ml_bi": nrm(ks[16], (DEPTH, ML_HEADS), 0.1),
        "ml_bf": jnp.linspace(3.0, 6.0, ML_HEADS, dtype=jnp.float32)[None, :] + nrm(ks[17], (DEPTH, ML_HEADS), 0.02),
        "ml_norm_g": gain(ks[18], (DEPTH, ML_W)),
        "w_out": nrm(ks[19], (DEPTH, MIX_W, D_MODEL), MIX_W ** -0.5),
        "xa_norm_g": gain(ks[20], (DEPTH, D_MODEL)),
        "mem_norm_g": gain(ks[21], (DEPTH, D_MODEL)),
        "xa_wq": nrm(ks[22], (DEPTH, D_MODEL, XA_W), D_MODEL ** -0.5),
        "xa_wkv": nrm(ks[23], (DEPTH, D_MODEL, 2 * XA_W), D_MODEL ** -0.5),
        "xa_wo": nrm(ks[24], (DEPTH, XA_W, D_MODEL), XA_W ** -0.5),
        "final_norm_g": gain(ks[25], (D_MODEL,)),
    }

def first_block(x, mem, mix_norm_g, w_in, lru_conv_w, lru_conv_b, lru_wa, lru_ba, lru_wx, lru_bx,
              lru_lambda, ml_conv_w, ml_conv_b, ml_wq, ml_wk, ml_wv, ml_bi, ml_bf, ml_norm_g,
              w_out, xa_norm_g, mem_norm_g, xa_wq, xa_wkv, xa_wo, final_norm_g):
    for l in range(DEPTH):
        h = rms_norm(x, mix_norm_g[l])
        p = h @ w_in[l]
        (lru_x, lru_z, ml_u, ml_o, ml_z, ml_i, ml_f,
         mo_q, mo_k, mo_v, mo_z) = jnp.split(p, SPLIT_POINTS, axis=-1)
        y_lru = rg_lru_branch(lru_x, lru_z, lru_conv_w[l], lru_conv_b[l], lru_wa[l], lru_ba[l],
                              lru_wx[l], lru_bx[l], lru_lambda[l])
        y_ml = mlstm_branch(ml_u, ml_o, ml_z, ml_i, ml_f, ml_conv_w[l], ml_conv_b[l], ml_wq[l],
                            ml_wk[l], ml_wv[l], ml_bi[l], ml_bf[l], ml_norm_g[l])
        y_mo = moba_branch(mo_q, mo_k, mo_v, mo_z)
        y = jnp.concatenate([y_lru, y_ml, y_mo], axis=-1)
        x = x + y @ w_out[l]
        hx = rms_norm(x, xa_norm_g[l])
        hm = rms_norm(mem, mem_norm_g[l])
        x = x + memory_cross_attention(hx, hm, xa_wq[l], xa_wkv[l], xa_wo[l])
    return rms_norm(x, final_norm_g)


N_MEM = 256
EPS = 1e-6
NEG = -1e30
POOL_WINDOWS = (2, 4, 8, 16)
POOL_GROUPS = 4
POOL_GW = D_MODEL // 8
POOL_W = POOL_GROUPS * POOL_GW
SWA_CONFIGS = ((128, 1), (512, 4), (2048, 16))
SWA_GROUPS = 3
SWA_HPG = 4
SWA_HEADS = SWA_GROUPS * SWA_HPG
HEAD_DIM = 128
SWA_QKV = SWA_HEADS * HEAD_DIM
SWA_OUT = SWA_HPG * HEAD_DIM
BLK = 128
GLA_HEADS = 4
GLA_DK = D_MODEL // 16
GLA_DV = D_MODEL // 8
GLA_K = GLA_HEADS * GLA_DK
GLA_V = GLA_HEADS * GLA_DV
GLA_RANK = 16
GLA_TAU = 16.0
GLA_CHUNK = 64
MEM_HEADS = 4
MEM_W = MEM_HEADS * HEAD_DIM
N_BRANCH = 4
IN_SPLITS = (POOL_W, POOL_W,
             SWA_QKV, SWA_QKV, SWA_QKV, SWA_OUT,
             GLA_K, GLA_K, GLA_V, GLA_V, GLA_RANK,
             MEM_W, MEM_W,
             N_BRANCH * D_MODEL)
D_IN = sum(IN_SPLITS)


def rms_norm_2(x, g):
    xf = x.astype(jnp.float32)
    y = xf * lax.rsqrt(jnp.mean(xf * xf, axis=-1, keepdims=True) + EPS)
    return (y * g.astype(jnp.float32)).astype(x.dtype)

def pool_mixer(u, gate, w_pool, scale):
    B, S, _ = u.shape
    ug = u.reshape(B, S, POOL_GROUPS, POOL_GW).astype(jnp.float32)
    cs = jnp.cumsum(ug, axis=1)
    cs0 = jnp.pad(cs, ((0, 0), (1, 0), (0, 0), (0, 0)))
    pos = jnp.arange(S)
    outs = []
    for g, w in enumerate(POOL_WINDOWS):
        hi = cs[:, :, g]
        lo = jnp.pad(cs0[:, :S - w + 1, g], ((0, 0), (w - 1, 0), (0, 0)))
        cnt = jnp.minimum(pos + 1, w).astype(jnp.float32)[None, :, None]
        outs.append((hi - lo) / cnt - ug[:, :, g])
    pooled = jnp.stack(outs, axis=2).astype(u.dtype)
    mixed = jnp.einsum('bsgc,gcd->bsgd', pooled, w_pool).reshape(B, S, POOL_W) * scale
    return mixed * jax.nn.silu(gate)

def dilated_window_attn(q, k, v, window, dilation, slopes):
    B, S, H, Dh = q.shape
    nk = window // dilation
    L = -(-S // (dilation * BLK)) * BLK
    pad = L * dilation - S
    nb = L // BLK

    def to_blocks(t):
        t = jnp.pad(t, ((0, 0), (0, pad), (0, 0), (0, 0)))
        t = t.reshape(B, L, dilation, H, Dh).transpose(0, 2, 1, 3, 4)
        return t.reshape(B, dilation, nb, BLK, H, Dh)

    def band(t):
        prev = jnp.pad(t[:, :, :-1], ((0, 0), (0, 0), (1, 0), (0, 0), (0, 0), (0, 0)))
        return jnp.concatenate([prev, t], axis=3)

    qb = to_blocks(q)
    kk = band(to_blocks(k))
    vv = band(to_blocks(v))
    s = jnp.einsum('brnqhd,brnkhd->brnhqk', qb, kk).astype(jnp.float32) * (Dh ** -0.5)
    qi = jnp.arange(BLK)[:, None]
    kj = jnp.arange(2 * BLK)[None, :] - BLK
    delta = qi - kj
    first = (jnp.arange(nb) == 0)[:, None, None]
    valid = (delta >= 0) & (delta <= nk) & ~(first & (kj < 0))
    bias = -slopes[:, None, None] * (delta * dilation).astype(jnp.float32)
    s = jnp.where(valid[None, None, :, None], s + bias[None, None, None], NEG)
    m = jnp.max(s, axis=-1, keepdims=True)
    e = jnp.exp(s - m)
    den = jnp.sum(e, axis=-1, keepdims=True)
    o = jnp.einsum('brnhqk,brnkhd->brnqhd', (e / den).astype(v.dtype), vv)
    lse = (m + jnp.log(den))[..., 0]
    o = o.reshape(B, dilation, L, H, Dh).transpose(0, 2, 1, 3, 4).reshape(B, L * dilation, H, Dh)[:, :S]
    lse = lse.transpose(0, 1, 2, 4, 3).reshape(B, dilation, L, H).transpose(0, 2, 1, 3)
    lse = lse.reshape(B, L * dilation, H)[:, :S]
    return o, lse

def swa_mixer(q, k, v, gate):
    B, S, _ = q.shape
    slopes = jnp.exp2(-8.0 * (jnp.arange(SWA_HEADS, dtype=jnp.float32) + 1.0) / SWA_HEADS)
    qg = q.reshape(B, S, SWA_GROUPS, SWA_HPG, HEAD_DIM)
    kg = k.reshape(B, S, SWA_GROUPS, SWA_HPG, HEAD_DIM)
    vg = v.reshape(B, S, SWA_GROUPS, SWA_HPG, HEAD_DIM)
    outs, lses = [], []
    for g, (w, d) in enumerate(SWA_CONFIGS):
        o_g, l_g = dilated_window_attn(qg[:, :, g], kg[:, :, g], vg[:, :, g], w, d,
                                       slopes[g * SWA_HPG:(g + 1) * SWA_HPG])
        outs.append(o_g)
        lses.append(l_g)
    o = jnp.stack(outs, axis=2)
    wts = jax.nn.softmax(jnp.stack(lses, axis=2), axis=2)
    o = jnp.sum(wts[..., None].astype(o.dtype) * o, axis=2).reshape(B, S, SWA_OUT)
    return o * jax.nn.silu(gate)

def gla_mixer(q, k, v, lr, gate, w_alpha, b_alpha, g_gla):
    B, S, _ = q.shape
    C = GLA_CHUNK
    nc = S // C
    f32 = jnp.float32
    z = (lr @ w_alpha + b_alpha).astype(f32)
    log_a = jax.nn.log_sigmoid(z) / GLA_TAU
    qc = q.astype(f32).reshape(B, nc, C, GLA_HEADS, GLA_DK) * (GLA_DK ** -0.5)
    kc = k.astype(f32).reshape(B, nc, C, GLA_HEADS, GLA_DK)
    vc = v.astype(f32).reshape(B, nc, C, GLA_HEADS, GLA_DV)
    bc = jnp.cumsum(log_a.reshape(B, nc, C, GLA_HEADS, GLA_DK), axis=2)
    b_last = bc[:, :, -1]
    q_t = qc * jnp.exp(bc)
    k_t = kc * jnp.exp(-bc)
    causal = jnp.tril(jnp.ones((C, C), dtype=bool))
    a = jnp.where(causal, jnp.einsum('bcihk,bcjhk->bchij', q_t, k_t), 0.0)
    o_intra = jnp.einsum('bchij,bcjhv->bcihv', a, vc)
    kv = jnp.einsum('bcjhk,bcjhv->bchkv', kc * jnp.exp(b_last[:, :, None] - bc), vc)
    decay = jnp.exp(b_last)

    def step(state, inp):
        dec, kv_c = inp
        return dec[..., None] * state + kv_c, state

    _, s_prev = lax.scan(step, jnp.zeros((B, GLA_HEADS, GLA_DK, GLA_DV), f32),
                         (decay.transpose(1, 0, 2, 3), kv.transpose(1, 0, 2, 3, 4)))
    s_prev = s_prev.transpose(1, 0, 2, 3, 4)
    o = o_intra + jnp.einsum('bcihk,bchkv->bcihv', q_t, s_prev)
    o = o.reshape(B, S, GLA_HEADS, GLA_DV)
    o = o * lax.rsqrt(jnp.mean(o * o, axis=-1, keepdims=True) + EPS)
    o = o.reshape(B, S, GLA_V) * g_gla.astype(f32)
    return o.astype(q.dtype) * jax.nn.silu(gate)

def mem_attn(q, gate, mem, g_mem, w_mem_kv):
    B, S, _ = q.shape
    kv = rms_norm_2(mem, g_mem) @ w_mem_kv
    km, vm = jnp.split(kv, 2, axis=-1)
    km = km.reshape(B, N_MEM, MEM_HEADS, HEAD_DIM)
    vm = vm.reshape(B, N_MEM, MEM_HEADS, HEAD_DIM)
    qh = q.reshape(B, S, MEM_HEADS, HEAD_DIM)
    s = jnp.einsum('bshd,bmhd->bhsm', qh, km).astype(jnp.float32) * (HEAD_DIM ** -0.5)
    p = jax.nn.softmax(s, axis=-1)
    o = jnp.einsum('bhsm,bmhd->bshd', p.astype(vm.dtype), vm).reshape(B, S, MEM_W)
    return o * jax.nn.silu(gate)

def second_inputs(seed: int = 0) -> dict:
    key = jax.random.key(seed)
    ks = jax.random.split(key, 20)
    f32 = jnp.float32
    nrm = lambda k, shape, scale: (jax.random.normal(k, shape, f32) * scale)
    return {
        'x': nrm(ks[0], (BATCH, SEQ, D_MODEL), 1.0),
        'mem': nrm(ks[1], (BATCH, N_MEM, D_MODEL), 1.0),
        'g_pre': 1.0 + nrm(ks[2], (DEPTH, D_MODEL), 0.05),
        'g_post': 1.0 + nrm(ks[3], (DEPTH, D_MODEL), 0.05),
        'g_mem': 1.0 + nrm(ks[4], (DEPTH, D_MODEL), 0.05),
        'w_in': nrm(ks[5], (DEPTH, D_MODEL, D_IN), D_MODEL ** -0.5),
        'b_merge': nrm(ks[6], (DEPTH, N_BRANCH, D_MODEL), 0.1),
        'w_pool': nrm(ks[7], (DEPTH, POOL_GROUPS, POOL_GW, POOL_GW), POOL_GW ** -0.5),
        'pool_scale': 1.0 + nrm(ks[8], (DEPTH, POOL_W), 0.05),
        'w_alpha': nrm(ks[9], (DEPTH, GLA_RANK, GLA_K), GLA_RANK ** -0.5),
        'b_alpha': nrm(ks[10], (DEPTH, GLA_K), 0.1),
        'g_gla': 1.0 + nrm(ks[11], (DEPTH, GLA_V), 0.05),
        'w_mem_kv': nrm(ks[12], (DEPTH, D_MODEL, 2 * MEM_W), D_MODEL ** -0.5),
        'w_br_pool': nrm(ks[13], (DEPTH, POOL_W, D_MODEL), POOL_W ** -0.5),
        'w_br_swa': nrm(ks[14], (DEPTH, SWA_OUT, D_MODEL), SWA_OUT ** -0.5),
        'w_br_gla': nrm(ks[15], (DEPTH, GLA_V, D_MODEL), GLA_V ** -0.5),
        'w_br_mem': nrm(ks[16], (DEPTH, MEM_W, D_MODEL), MEM_W ** -0.5),
        'w_out': nrm(ks[17], (DEPTH, D_MODEL, D_MODEL), D_MODEL ** -0.5),
    }

def second_block(x, mem, g_pre, g_post, g_mem, w_in, b_merge, w_pool, pool_scale, w_alpha, b_alpha,
              g_gla, w_mem_kv, w_br_pool, w_br_swa, w_br_gla, w_br_mem, w_out):
    B, S, _ = x.shape
    split_at = np.cumsum(IN_SPLITS)[:-1]
    for l in range(DEPTH):
        h = rms_norm_2(x, g_pre[l])
        proj = h @ w_in[l]
        (a_val, a_gate, sq, sk, sv, s_gate, cq, ck, cv, c_gate, c_lr,
         mq, m_gate, g_logits) = jnp.split(proj, split_at, axis=-1)
        y_a = pool_mixer(a_val, a_gate, w_pool[l], pool_scale[l])
        y_b = swa_mixer(sq, sk, sv, s_gate)
        y_c = gla_mixer(cq, ck, cv, c_lr, c_gate, w_alpha[l], b_alpha[l], g_gla[l])
        y_m = mem_attn(mq, m_gate, mem, g_mem[l], w_mem_kv[l])
        gates = jax.nn.sigmoid(g_logits.reshape(B, S, N_BRANCH, D_MODEL) + b_merge[l])
        merged = (gates[:, :, 0] * (y_a @ w_br_pool[l]) + gates[:, :, 1] * (y_b @ w_br_swa[l])
                  + gates[:, :, 2] * (y_c @ w_br_gla[l]) + gates[:, :, 3] * (y_m @ w_br_mem[l]))
        x = x + rms_norm_2(merged @ w_out[l], g_post[l])
    return x


def setup_inputs(seed=0):
    out = dict(first_inputs(seed))
    for name, value in second_inputs(seed + 1).items():
        if name != "x":
            out[name + "_2"] = value
    return out


def reference(
    x, mem, mix_norm_g, w_in, lru_conv_w, lru_conv_b, lru_wa, lru_ba, lru_wx, lru_bx,
    lru_lambda, ml_conv_w, ml_conv_b, ml_wq, ml_wk, ml_wv, ml_bi, ml_bf, ml_norm_g, w_out,
    xa_norm_g, mem_norm_g, xa_wq, xa_wkv, xa_wo, final_norm_g, mem_2, g_pre_2, g_post_2,
    g_mem_2, w_in_2, b_merge_2, w_pool_2, pool_scale_2, w_alpha_2, b_alpha_2, g_gla_2,
    w_mem_kv_2, w_br_pool_2, w_br_swa_2, w_br_gla_2, w_br_mem_2, w_out_2,
):
    x = first_block(
        x, mem, mix_norm_g, w_in, lru_conv_w, lru_conv_b, lru_wa, lru_ba, lru_wx, lru_bx,
        lru_lambda, ml_conv_w, ml_conv_b, ml_wq, ml_wk, ml_wv, ml_bi, ml_bf, ml_norm_g, w_out,
        xa_norm_g, mem_norm_g, xa_wq, xa_wkv, xa_wo, final_norm_g,
    )
    return second_block(
        x, mem_2, g_pre_2, g_post_2, g_mem_2, w_in_2, b_merge_2, w_pool_2, pool_scale_2,
        w_alpha_2, b_alpha_2, g_gla_2, w_mem_kv_2, w_br_pool_2, w_br_swa_2, w_br_gla_2,
        w_br_mem_2, w_out_2,
    )


_drawn_inputs = setup_inputs


def setup_inputs(seed=0):
    import zlib

    import numpy as np

    out = dict(_drawn_inputs(seed))
    spreads = {}
    factors = {'lru_ba': 8.0,
     'lru_bx': 8.0,
     'ml_conv_b': 3.846,
     'ml_bi': 8.0,
     'ml_norm_g': 5.972,
     'xa_norm_g': 8.0,
     'mem_norm_g': 8.0,
     'g_mem_2': 8.0,
     'pool_scale_2': 21.849,
     'w_alpha_2': 4.757,
     'b_alpha_2': 8.0,
     'g_gla_2': 8.0,
     'w_br_swa_2': 3.183}
    for name, (base, spread) in spreads.items():
        noise = np.random.default_rng([zlib.crc32(name.encode()), seed]).standard_normal(out[name].shape)
        drawn = base * np.exp(spread * noise) if base else spread * noise
        out[name] = jnp.asarray(drawn.astype(out[name].dtype))
    for name, factor in factors.items():
        out[name] = (out[name] * factor).astype(out[name].dtype)
    return out
```

```python
from contextlib import ExitStack

import concourse.bass as bass
from concourse import mybir

ALU = mybir.AluOpType
ACT = mybir.ActivationFunctionType
AX = mybir.AxisListType.X
F32 = mybir.dt.float32
F32R = mybir.dt.float32r
U32 = mybir.dt.uint32

P = 128
T = 512
NT = T // P
D = 2048
KT = D // P
M = 256
RMS_EPS = 1e-6
LN_EPS = 1e-5
MASKED = -1e33

LRU_W, ML_W, MO_W = 512, 768, 768
C_LRU_X, C_LRU_Z = 0, 512
C_ML_U, C_ML_O, C_ML_Z, C_ML_I = 1024, 1792, 2560, 3328
C_MO_Q, C_MO_K, C_MO_V, C_MO_Z = 3336, 4104, 4872, 5640
C_POOL_V, C_POOL_G = 0, 1024
C_SQ, C_SK, C_SV, C_SG = 2048, 3584, 5120, 6656
C_GQ, C_GK, C_GV, C_GG, C_GLR = 7168, 7680, 8192, 9216, 10240
C_MQ, C_MG, C_GATE = 10256, 10768, 11280

LRU_BLOCKS = 4
ML_PAIRS, ML_DH, ML_TILES = 2, 192, 3
MO_HEADS, XA_HEADS, SWA_GROUPS, SWA_HPG, MEM_HEADS = 6, 4, 3, 4, 4
GLA_HEADS, GLA_DK, GLA_DV, GLA_CHUNK = 4, 128, 256, 64
POOL_GROUPS = 4
HEAD_SCALE = 128.0 ** -0.5
MO_SLOPES = [2.0 ** -2, 2.0 ** -4, 2.0 ** -6, 2.0 ** -8, 2.0 ** -1, 2.0 ** -3]
SWA_SLOPES = [2.0 ** (-8.0 * (h + 1) / 12) for h in range(12)]

RING = 4
HALF = 8 * P
PHASES = [("kv", 32, 16), ("lru", 16, 8), ("mlg", 4, 0), ("ml", 36, 18), ("moba", 48, 24), ("wout", 32, 16),
          ("xq", 8, 4), ("xwo", 8, 16), ("glr", 4, 0), ("gla", 48, 24), ("merge_g", 48, 32), ("swa", 80, 40),
          ("mem", 16, 8), ("merge_sm", 80, 64), ("pool", 32, 16), ("merge_p", 48, 32), ("wout2", 32, 16)]
H4, Q2 = {}, {}
_h = _q = 0
for _name, _dh, _dq in PHASES:
    H4[_name], Q2[_name] = _h // RING, _q // 2
    _h, _q = _h + _dh, _q + _dq
NH = _h
assert NH % RING == 0

PARAM = {}
STACKS = [[("mix_norm_g", 16), ("xa_norm_g", 16), ("mem_norm_g", 16), ("final_norm_g", 16),
           ("g_pre", 16), ("g_post", 16), ("g_mem", 16)],
          [("lru_conv_w", 16), ("lru_conv_b", 4), ("lru_ba", 4), ("lru_bx", 4), ("lru_lambda", 4),
           ("ml_conv_w", 24), ("ml_conv_b", 6), ("ml_norm_g", 6), ("pool_scale", 8), ("b_alpha", 4),
           ("g_gla", 8)],
          [("b_merge", 64)]]
_c = 0
for _s in STACKS:
    for _name, _n in _s:
        PARAM[_name] = _c
        _c += _n
NPARAM = _c


CAUSAL = [(0, t + 1) for t in range(NT)]
WINDOW = [(max(t - 1, 0), min(t + 1, 2)) for t in range(NT)]
FULL = [(0, 2)] * NT


class Events:

    def __init__(self, sem, names):
        self.sem, self.names = sem, names.split()
        assert len(set(self.names)) == len(self.names)

    def value(self, name, task=0):
        return task * len(self.names) + self.names.index(name) + 1


class Chain:

    def __init__(self, eng, sem):
        self.eng, self.sem, self.base, self.n = eng, sem, 0, 0

    def __call__(self, ins):
        ins.then_inc(self.sem, 1)
        self.n += 1
        self.eng.wait_ge(self.sem, self.base + self.n)

    def inc(self, ins):
        ins.then_inc(self.sem, 1)
        self.n += 1

    def enter(self, i, per):
        self.before = self.base + self.n
        self.per, self.base, self.n = per, self.before + i * per, 0

    def leave(self, count):
        assert self.n == self.per, f"{self.n} links in the loop's body, {self.per} given"
        self.base, self.n = self.before + count * self.per, 0


def build(nc, a, out, stop=None):
    with ExitStack() as ctx:
        base = (nc.sbuf_base + 63) // 64 * 64
        place = [base]

        def take(size):
            at = place[0]
            place[0] += (size + 63) // 64 * 64
            return at

        def at(name, shape, offset, dt=F32):
            return nc.alloc_sbuf_tensor_at(name, shape, dt, offset=offset)

        def keep(name, shape, dt=F32):
            n = 4
            for d in shape[1:]:
                n *= d
            return at(name, shape, take(n), dt)

        class Region:

            def __init__(self, *stretches):
                self.stretches = [list(s) for s in stretches]

            def __call__(self, name, shape, dt=F32):
                n = 4
                for d in shape[1:]:
                    n *= d
                n = (n + 63) // 64 * 64
                for s in self.stretches:
                    if s[0] + n <= s[1]:
                        s[0] += n
                        return at(name, shape, s[0] - n, dt)
                raise ValueError(f"no room for {name}: {n} in {self.stretches}")

        raw = keep("raw", [P, RING, HALF])
        w_hi = keep("w_hi", [P, RING, HALF], F32R)
        w_lo = keep("w_lo", [P, RING, HALF], F32R)
        ht_hi_at, ht_lo_at = take(KT * T * 4), take(KT * T * 4)
        ht_hi = at("ht_hi", [P, KT, T], ht_hi_at, F32R)
        ht_lo = at("ht_lo", [P, KT, T], ht_lo_at, F32R)
        xy_at = take(KT * T * 4)
        xy = at("xy", [P, KT, T], xy_at)
        kv1_at = take(8192)
        k1, v1 = at("k1", [P, 4, M], kv1_at), at("v1", [P, 4, 2, P], kv1_at + 4096)
        kv2_at = take(8192)
        k2, v2 = at("k2", [P, 4, M], kv2_at), at("v2", [P, 4, 2, P], kv2_at + 4096)
        dist = keep("dist", [P, T])
        ident = keep("ident", [P, P])
        ones = keep("ones", [P, P])
        par = keep("par", [P, NPARAM])
        sel = keep("sel", [2, 2, P])
        small = keep("small", [P, 48])
        count16 = keep("count16", [P, 16])
        gate_bias = keep("gate_bias", [2, 4])
        m_at = place[0]
        m_end = nc.sbuf_usable_end // 64 * 64

        def col(name, k=0):
            return par[:, PARAM[name] + k:PARAM[name] + k + 1]

        eps_rms, eps_ln = small[:, 0:1], small[:, 1:2]
        mo_slopes, swa_slopes = small[:, 2:8], small[:, 8:20]
        lru_half_c, lru_hba, lru_hbx = small[:, 20:24], small[:, 24:28], small[:, 28:32]

        def psum(name):
            return ctx.enter_context(nc.psum_tensor(name, [P, 512], F32))

        proj = [psum("proj0"), psum("proj1")]
        S = [psum(f"s{i}") for i in range(4)]
        TB = [psum("t0"), psum("t1")]

        def sem(name):
            return ctx.enter_context(nc.semaphore(name))

        raw_ready = [sem(f"raw_ready{i}") for i in range(RING)]
        mem_half_ready = sem("mem_half_ready")
        hi_done, lo_done, half_done = sem("hi_done"), sem("lo_done"), sem("half_done")
        part_done = sem("part_done")
        bank_free = [sem("bank_free0"), sem("bank_free1")]
        ht_ready, yh_ready = sem("ht_ready"), sem("yh_ready")
        dve_chain, act_chain = sem("dve_chain"), sem("act_chain")
        dve_phase, act_phase = sem("dve_phase"), sem("act_phase")
        params_in, consts_built = sem("params_in"), sem("consts_built")
        mem_in = [sem(f"mem_in{t}") for t in range(4)]
        x_in, weights_in, mem_scaled = sem("x_in"), sem("weights_in"), sem("mem_scaled")
        spilled, out_done = sem("spilled"), sem("out_done")
        tile_in = [sem("tile_in0"), sem("tile_in1")]

        def events(name, names):
            return Events(sem(name), names)

        x_spill = nc.dram_tensor("x_spill", (KT, P, T), F32, kind="Internal").ap()
        x2_spill = nc.dram_tensor("x2_spill", (KT, P, T), F32, kind="Internal").ap()
        root_spill = nc.dram_tensor("root_spill", (P, T), F32, kind="Internal").ap()

        def wait(eng, ev, name, task=0):
            eng.wait_ge(ev.sem, ev.value(name, task))

        pro = Region((m_at, m_end))
        mem_tok = pro("mem_tok", [P, 4, D])
        x_t = at("x_t", [P, KT, T], m_at)
        kv_v = at("kv_v", [P, M], pro.stretches[0][0])
        stack = [pro(f"stack{i}", [P, P]) for i in range(3)]
        lru_wa, lru_wx = pro("lru_wa", [P, 4, P]), pro("lru_wx", [P, 4, P])
        x_tok = at("x_tok", [P, NT, D], xy_at)
        mem_ss, mem_rstd = small[:, 38:42], small[:, 42:46]
        p_acc, p_sq = pro("p_acc", [P, T]), pro("p_sq", [P, T])
        unread = [at("unread0", [P, D], kv1_at), at("unread1", [P, D], kv2_at)]
        up_xy = Region((xy_at + 10 * 2048, xy_at + 16 * 2048))
        n0 = [up_xy(f"n0_{i}", [P, T]) for i in range(6)]

        lru = Region((m_at, m_at + 32768))
        l_xp = lru("l_xp", [P, 3 + T])
        l_w = lru("l_w", [P, 2, P])
        l_xc, l_tr, l_ti, l_t, l_rd, l_q, l_a, l_s, l_h, l_tz, l_sz = [
            lru(f"l_{n}", [P, T]) for n in "xc tr ti t rd q a s h tz sz".split()]

        ml = Region((m_at, m_end))
        m_bd = ml("m_bd", [P, 3, 3, P])
        m_up, m_uc = ml("m_up", [P, 3 + T]), ml("m_uc", [P, T])
        m_q, m_k = ml("m_q", [P, 4, T]), ml("m_k", [P, 3, T])
        m_v = ml("m_v", [P, NT, 2, ML_DH + 1])
        m_h = ml("m_h", [P, NT, 2, ML_DH])
        m_e = ml("m_e", [P, 2, P])
        m_kt = ml("m_kt", [P, 2, ML_DH])
        m_c = ml("m_c", [P, 3, ML_DH + 1])
        m_tot = ml("m_tot", [P, 2, ML_DH + 1])
        m_sm = ml("m_sm", [P, 64])
        m_neg = ml("m_neg", [P, P])
        m_wd, m_bdmask = at("m_wd", [P, 3, 6, 4], xy_at + 7 * 2048), at("m_bdmask", [P, P], xy_at + 8 * 2048)
        mr = Region((xy_at + 10 * 2048, xy_at + 16 * 2048))
        r_ig, r_f, r_b, r_r = [mr(f"r_{n}", [P, T]) for n in "ig f b r".split()]
        m_g, m_gc = mr("m_g", [P, T]), mr("m_gc", [P, NT, P])
        m_vc = m_uc

        mo = Region((m_at, m_end))
        a_v, a_q, a_k, a_vt, a_z = [mo(f"a_{n}", [P, T]) for n in "v q k vt z".split()]
        a_l, a_pt = mo("a_l", [P, 1280]), mo("a_pt", [P, 1280])
        a_o = mo("a_o", [P, T])
        a_st = mo("a_st", [P, 12])
        a_strip = mo("a_strip", [P, T])

        nrm = Region((m_at, m_end))
        n_acc, n_rstd, n_sq, n_t0, n_t1, n_x0, n_x1 = [
            nrm(f"n_{n}", [P, T]) for n in "acc rstd sq t0 t1 x0 x1".split()]
        b_q, b_o = nrm("b_q", [P, T]), nrm("b_o", [P, T])
        b_st = nrm("b_st", [P, 12])
        b_l, b_pt = nrm("b_l", [P, 1024]), nrm("b_pt", [P, 1024])
        o_hi, o_lo = nrm("o_hi", [P, 4, T], F32R), nrm("o_lo", [P, 4, T], F32R)

        gl = Region((xy_at, xy_at + 32768), (m_at + 32768, m_end), (kv1_at, kv1_at + 8192))
        g_st = gl("g_st", [P, 7, GLA_DV])
        g_x, g_b, g_e, g_qt, g_kt, g_kk, g_v = [gl(f"g_{n}", [P, T]) for n in "x b e qt kt kk v".split()]
        g_vt, g_o = gl("g_vt", [P, NT, GLA_DV]), gl("g_o", [P, NT, GLA_DV])
        g_kkt, g_at, g_mask = [gl(f"g_{n}", [P, NT, P]) for n in "kkt at mask".split()]
        g_z = gl("g_z", [P, 2, T])
        g_y = gl("g_y", [P, T])
        g_wh = gl("g_wh", [16, P])
        g_lr, g_wal = gl("g_lr", [16, T]), gl("g_wal", [16, T])
        g_dec = gl("g_dec", [P, 8])
        g_ss = gl("g_ss", [P, 8])

        mg = Region((m_at + 32768, m_end))
        e_th, e_tmp = [mg("e_th0", [P, T]), mg("e_th1", [P, T])], mg("e_tmp", [P, T])
        yh = at("yh", [P, 8, T], m_at, F32R)
        yl = at("yl", [P, 8, T], m_at + 16384, F32R)

        sw = Region((m_at + 8192, m_at + 16384), (m_at + 24576, m_end), (kv1_at, kv1_at + 8192))
        w_og = sw("w_og", [P, 3, T])
        w_l, w_pt = sw("w_l", [P, 1280]), sw("w_pt", [P, 1280])
        w_v, w_q, w_k, w_vt = [sw(f"w_{n}", [P, T]) for n in "v q k vt".split()]
        w_strip4, w_strip16 = sw("w_strip4", [P, T]), sw("w_strip16", [P, T])
        w_strip1 = sw("w_strip1", [P, M])
        w_st = sw("w_st", [P, 48])
        po = Region((m_at + 32768, m_end), (kv1_at, kv1_at + 8192), (kv2_at, kv2_at + 8192))
        p_w = at("p_w", [P, 4, 2, 2, P], kv1_at)
        po.stretches.pop(1)
        p_u = [po(f"p_u{i}", [P, 16 + T]) for i in range(2)]
        p_s = [po(f"p_s{i}", [P, 16 + T]) for i in range(2)]
        p_p = [po(f"p_p{i}", [P, T]) for i in range(2)]
        p_z, p_rc = po("p_z", [P, T]), po("p_rc", [P, 4, 16])
        mm = Region((m_at + 32768, m_end), (kv1_at, kv1_at + 8192))
        c_q, c_z, c_o, c_y = [mm(f"c_{n}", [P, T]) for n in "q z o y".split()]
        c_st = mm("c_st", [P, 12])
        c_l = at("c_l", [P, 1024], kv1_at)
        c_pt = at("c_pt", [P, 1024], kv1_at + 4096)

        n_acc3, n_sq3, n_rs = n_x0, n_x1, b_q
        x3 = at("x3", [P, KT, T], m_at)
        fi = Region((kv1_at, kv1_at + 16384))
        f_acc, f_rstd, f_sq, f_rs = [fi(f"f_{n}", [P, T]) for n in "acc rstd sq rs".split()]

        w1, w2 = a["w_in"][0], a["w_in_2"][0]
        HT_MEM, HT_X, HT_Y, HT_X1, HT_H2, HT_MERGED = range(0, 6 * KT, KT)
        Z_X, Z_X1, Z_X2, _, Z_Y2 = range(0, 5 * KT, KT)
        YH_XA, YH_GLA, YH_SWA, YH_MEM, YH_POOL, YH_END = 0, 4, 12, 16, 20, 28
        A_MO, A_XA, A_SWA, A_MEM = 0, 6, 10, 22

        def ready(n):
            return not isinstance(n, int) or n > 0

        def need(eng, s, n):
            if ready(n):
                eng.wait_ge(s, n)

        att_s, att_l, att_e, att_p, att_c = [sem(f"att_{n}") for n in
                                             "scores logits exps probs_t probs_copied".split()]
        att_o, att_ok, att_ot, att_y, att_vt, att_vc = [sem(f"att_{n}") for n in
                                                        "out out_kept out_t y v_t v_copied".split()]
        att_k = sem("att_k")
        norm_sum, norm_root, norm_t, norm_hi = [sem(f"norm_{n}") for n in "sum root t hi".split()]
        norm_sq, norm_acc = sem("norm_sq"), sem("norm_acc")
        pro_pe, pro_act, pro_dve = events("pro_pe", "params"), events("pro_act", "sq root"), \
            events("pro_dve", "params rstd")
        memt_pe, memt_hi = sem("memt_pe"), sem("memt_hi")
        xt_pe, xt_x = sem("xt_pe"), sem("xt_x")
        kv_t = sem("kv_t")
        v1_done = sem("v1_done")
        lru_pe, lru_act, lru_dve = events("lru_pe", "gates"), events("lru_act", "i t z root"), \
            events("lru_dve", "xc s y")
        ml_pe = events("ml_pe", "gates qk0 v0 qk1 g sold v1 qk2 v2 o0 o1 o2 st0 kt0 num0 cu0 "
                       "st1 kt1 num1 cu1 st2 kt2 num2 cu2 st3 num3 y0 y1 y2")
        ml_act = events("ml_act", "ln th0 q0 rows th1 vt0 q1 th2 gc vt1 q2 o0 vt2 o1 o2 "
                        "e0 z0 kts0 tot0 e1 z1 z2 kts1 tot1 e2 kts2 tot2 e3 tot3 root")
        ml_dve = events("ml_dve", "uc0 rows k0 v0 uc1 k1 v1 uc2 sold k2 v2 ot0 ot1 ot2 "
                        "se0 c0 se1 c1 se2 c2 se3 hn y")
        gla_pe = events("gla_pe", "z kk va vb at kv o ot")
        gla_wh = sem("gla_wh")
        gla_act = events("gla_act", "ln ex kkt z0 z1 sq root hi0 hi1")
        gla_dve = events("gla_dve", "bc kt kk va vb at st o y0 y1")
        comb_act = events("comb_act", "z w")
        comb_dve = events("comb_dve", "m")
        mem_act = events("mem_act", "z")
        moz_act = events("moz_act", "z")
        merge_th = [sem("merge_th0"), sem("merge_th1")]
        pool_pe, pool_act, pool_dve = events("pool_pe", "mix"), events("pool_act", "z0 hi0 z1 hi1"), \
            events("pool_dve", "p y0 y1")
        ml_gate, ml_conv, ml_var = events("ml_gate", "rows"), sem("ml_conv"), sem("ml_var")
        yh_f, yh_hi, y2_tile, comb_in = [sem(n) for n in "yh_f yh_hi y2_tile comb_in".split()]
        merged_done, lru_c, lru_lam = sem("merged_done"), sem("lru_c"), sem("lru_lam")
        n_x = [n_x0, n_x1]
        gate_rows = xy[:, 9, :]
        m_hf = m_h[:].rearrange("p c h d -> p (c h d)")
        m_hr = m_h[:].rearrange("p c h d -> p c (h d)")
        m_mv = m_sm[:, 32:48].rearrange("p (k s) -> p k s", s=2)
        w_wt = w_st[:, 36:48]
        fin_pe, fin_copy, fin_dve = sem("fin_pe"), sem("fin_copy"), sem("fin_dve")
        NPAR_DMA = sum(len(x) for x in STACKS) + 2
        CONSTS = 9 + len(MO_SLOPES) + len(SWA_SLOPES)
        x2_done, norm_v, x2_in = sem("x2_done"), sem("norm_v"), sem("x2_in")
        y_tok = at("y_tok", [P, NT, D], ht_hi_at)

        def th(b, j):
            return 4 * b + j + 1

        def gla_kv(c):
            bank = (S[1], S[2], S[3], TB[1])[2 * (c % 2) + c // 4]
            x = (c // 2) % 2
            return bank[:, x * GLA_DV:(x + 1) * GLA_DV]

        block = ctx.enter_context(nc.Block())

        @block.sync
        def _(sp):
            def half(b, j, src, n=P, ks=8, off=0, s=None):
                slot = j % RING
                if s is None:
                    need(sp, lo_done, th(b, j) - RING)
                dst = raw[:, slot, :].rearrange("p (k n) -> p k n", n=P)[:, off:off + ks, 0:n]
                sp.dma_start(dst, src.rearrange("(k p) n -> p k n", p=P)).then_inc(
                    raw_ready[slot] if s is None else s, 16)

            def unit(b, j, w, c):
                half(b, j, w[0:1024, bass.ds(c, P)])
                half(b, j + 1, w[1024:2048, bass.ds(c, P)])

            def loop(name, count, per, body):
                with sp.Fori(1, count + 1) as i:
                    body(H4[name] + (i - 1) * (per // RING), i - 1)

            for t in range(4):
                src = a["mem" if t < 2 else "mem_2"][0][(t % 2) * P:(t % 2 + 1) * P, :]
                sp.dma_start(mem_tok[:, t, :], src).then_inc(mem_in[t], 16)
            named = {"mix_norm_g": a["mix_norm_g"][0], "xa_norm_g": a["xa_norm_g"][0],
                     "mem_norm_g": a["mem_norm_g"][0], "final_norm_g": a["final_norm_g"],
                     "g_pre": a["g_pre_2"][0], "g_post": a["g_post_2"][0], "g_mem": a["g_mem_2"][0],
                     "lru_conv_w": a["lru_conv_w"][0].rearrange("j c -> (j c)"), "lru_conv_b": a["lru_conv_b"][0],
                     "lru_ba": a["lru_ba"][0], "lru_bx": a["lru_bx"][0], "lru_lambda": a["lru_lambda"][0],
                     "ml_conv_w": a["ml_conv_w"][0].rearrange("j c -> (j c)"), "ml_conv_b": a["ml_conv_b"][0],
                     "ml_norm_g": a["ml_norm_g"][0], "pool_scale": a["pool_scale_2"][0],
                     "b_alpha": a["b_alpha_2"][0], "g_gla": a["g_gla_2"][0],
                     "b_merge": a["b_merge_2"][0].rearrange("b c -> (b c)")}
            for s, names in enumerate(STACKS):
                r = 0
                for name, n in names:
                    sp.dma_start(stack[s][r:r + n, :], named[name].rearrange("(k p) -> k p", p=P)).then_inc(params_in, 16)
                    r += n
            sp.dma_start(gate_bias[:, 0:2], a["ml_bi"][0].rearrange("(p h) -> h p", h=2),
                         allow_slow_non_contiguous=True).then_inc(params_in, 16)
            sp.dma_start(gate_bias[:, 2:4], a["ml_bf"][0].rearrange("(p h) -> h p", h=2),
                         allow_slow_non_contiguous=True).then_inc(params_in, 16)

            wkv = [a["xa_wkv"][0], a["w_mem_kv_2"][0]]
            unit(0, 0, wkv[0], 0)
            unit(0, 2, wkv[0], 512)
            sp.dma_start(x_tok[:], a["x"][0].rearrange("(t p) d -> p t d", p=P)).then_inc(x_in, 16)
            sp.dma_start(lru_wa[:], a["lru_wa"][0].rearrange("g i o -> i g o")).then_inc(weights_in, 16)
            sp.dma_start(lru_wx[:], a["lru_wx"][0].rearrange("g i o -> i g o")).then_inc(weights_in, 16)
            for src in range(2):
                with sp.Fori(1 - src, 4) as i:
                    unit(4 * src + i, 0, wkv[src], i * P)
                    unit(4 * src + i, 2, wkv[src], i * P + 512)

            def lru_loads(b, i):
                unit(b, 0, w1, i * P + C_LRU_X)
                unit(b, 2, w1, i * P + C_LRU_Z)
            sp.wait_ge(xt_x, KT)
            sp.dma_start(x_spill.rearrange("k p t -> p k t"), x_t[:]).then_inc(spilled, 16)
            loop("lru", LRU_BLOCKS, 4, lru_loads)

            for q in range(4):
                half(H4["mlg"], q, w1[512 * q:512 * q + 512, C_ML_I:C_ML_I + 8], n=8, ks=4)
            for pair in range(ML_PAIRS):
                for u in range(9):
                    c = (C_ML_U, C_ML_O, C_ML_Z)[u // 3] + 384 * pair + P * (u % 3)
                    unit(H4["ml"], 18 * pair + 2 * u, w1, c)

            def moba_loads(b, i):
                for u, c in enumerate((C_MO_V, C_MO_Q, C_MO_K, C_MO_Z)):
                    unit(b, 2 * u, w1, i * P + c)
            loop("moba", MO_HEADS, 8, moba_loads)

            def wide_loads(name, w, per):
                def body(b, i):
                    for u in range(per):
                        unit(b, 2 * u, w, i * per * P + u * P)
                return body
            loop("wout", KT // 2, 4, wide_loads("wout", a["w_out"][0], 2))
            for h in range(XA_HEADS):
                unit(H4["xq"], 2 * h, a["xa_wq"][0], h * P)

            def pairs(b, j, w, c):
                slot = j % RING
                src = w[:, bass.ds(c, 2 * P)].rearrange("(k p) n -> p k n", p=P)
                sp.wait_ge(lo_done, th(b, j) - RING)
                sp.dma_start(raw[:, slot, :].rearrange("p (k n) -> p k n", n=2 * P), src).then_inc(
                    raw_ready[slot], 16)

            def xwo_loads(b, i):
                for j in range(RING):
                    pairs(b, j, a["xa_wo"][0], i * 8 * P + j * 2 * P)
            loop("xwo", 2, 4, xwo_loads)
            for q in range(4):
                half(H4["glr"], q, w2[512 * q:512 * q + 512, C_GLR:C_GLR + 16], n=16, ks=4)
            sp.wait_ge(x2_done, 1)
            sp.dma_start(x2_spill.rearrange("k p t -> p k t"), xy[:]).then_inc(spilled, 16)
            def gla_loads(b, i):
                unit(b, 0, w2, i * P + C_GQ)
                unit(b, 2, w2, i * P + C_GK)
                for x in range(2):
                    unit(b, 4 + 2 * x, w2, i * 2 * P + C_GV + x * P)
                for x in range(2):
                    unit(b, 8 + 2 * x, w2, i * 2 * P + C_GG + x * P)
            loop("gla", GLA_HEADS, 12, gla_loads)

            def merge_loads(w_branch, branch):
                def body(b, i):
                    for t in range(4):
                        unit(b, 3 * t, w2, i * 4 * P + C_GATE + branch * D + t * P)
                        half(b, 3 * t + 2, w_branch[:, bass.ds((i * 4 + t + 1) * P - P, P)])
                return body
            loop("merge_g", 4, 12, merge_loads(a["w_br_gla_2"][0], 2))

            def swa_loads(b, i):
                for g in range(SWA_GROUPS):
                    for u, c in enumerate((C_SV, C_SQ, C_SK)):
                        unit(b, 6 * g + 2 * u, w2, i * P + c + g * SWA_HPG * P)
                unit(b, 18, w2, i * P + C_SG)
            loop("swa", SWA_HPG, 20, swa_loads)

            def mem_loads(b, i):
                unit(b, 0, w2, i * P + C_MQ)
                unit(b, 2, w2, i * P + C_MG)
            loop("mem", MEM_HEADS, 4, mem_loads)

            def merge_sm_loads(b, i):
                for t in range(4):
                    unit(b, 5 * t, w2, i * 4 * P + C_GATE + 1 * D + t * P)
                    unit(b, 5 * t + 2, w2, i * 4 * P + C_GATE + 3 * D + t * P)
                    half(b, 5 * t + 4, a["w_br_swa_2"][0][:, bass.ds((i * 4 + t + 1) * P - P, P)], ks=4)
                    half(b, 5 * t + 4, a["w_br_mem_2"][0][:, bass.ds(i * 4 * P + t * P, P)], ks=4, off=4,
                         s=mem_half_ready)
            loop("merge_sm", 4, 20, merge_sm_loads)
            for g in range(POOL_GROUPS):
                for u in range(4):
                    c = (C_POOL_V, C_POOL_G)[u // 2] + 2 * g * P + (u % 2) * P
                    unit(H4["pool"], 8 * g + 2 * u, w2, c)
            loop("merge_p", 4, 12, merge_loads(a["w_br_pool_2"][0], 0))
            loop("wout2", KT // 2, 4, wide_loads("wout2", a["w_out_2"][0], 2))
            for q in range(4):
                sp.wait_ge(fin_copy, 4 * q + 4)
                sp.dma_start(out[0].rearrange("(t p) d -> p t d", p=P)[:, :, 512 * q:512 * q + 512],
                             y_tok[:, :, 512 * q:512 * q + 512]).then_inc(out_done, 16)
            sp.wait_ge(out_done, 64)

        @block.gpsimd
        def _(pool):
            made = [0]

            def make(ins, wait=False):
                ins.then_inc(consts_built, 1)
                made[0] += 1
                if wait:
                    pool.wait_ge(consts_built, made[0])

            make(pool.memset(ident[:], 0.0), True)
            make(pool.affine_select(out=ident[:], in_=ident[:], compare_op=ALU.not_equal, fill=1.0, base=0,
                                    pattern=[[-1, P]], channel_multiplier=1))
            make(pool.memset(ones[:], 1.0))
            make(pool.iota(dist[:], [[1, T]], base=-(T - P), channel_multiplier=-1,
                           allow_small_or_imprecise_dtypes=True))
            make(pool.iota(count16[:], [[1, 16]], base=1, channel_multiplier=0,
                           allow_small_or_imprecise_dtypes=True))
            make(pool.memset(sel[:], 1.0), True)
            make(pool.affine_select(out=sel[:], in_=sel[:], compare_op=ALU.is_equal, fill=0.0, base=0,
                                    pattern=[[-1, 2], [0, P]], channel_multiplier=1))
            make(pool.memset(eps_rms, RMS_EPS))
            make(pool.memset(eps_ln, LN_EPS))
            for k, v in enumerate(MO_SLOPES):
                make(pool.memset(mo_slopes[:, k:k + 1], v))
            for k, v in enumerate(SWA_SLOPES):
                make(pool.memset(swa_slopes[:, k:k + 1], v))
            assert made[0] == CONSTS

            with pool.Fori(0, NH // RING) as i:
                for slot in range(RING):
                    pool.wait_ge(hi_done, i * RING + slot + 1)
                    pool.tensor_tensor(w_lo[:, slot, :], raw[:, slot, :], w_hi[:, slot, :].bitcast(F32),
                                       ALU.subtract).then_inc(lo_done, 1)

        @block.tensor
        def _(pe):
            def bank_wait(b, q):
                need(pe, bank_free[q % 2], b + q // 2)

            def accumulate(b, j, dst, kts, kk, hi, lo, cols, first, last, fresh=None, done=True, step=1):
                slot = j % RING
                pe.wait_ge(lo_done, th(b, j))
                for n, kt in enumerate(kts):
                    if fresh is not None:
                        pe.wait_ge(fresh[0], fresh[1] + kt + 1)
                    wh = w_hi[:, slot, (kk + n * step) * P:(kk + n * step + 1) * P]
                    wl = w_lo[:, slot, (kk + n * step) * P:(kk + n * step + 1) * P]
                    c0, c1 = cols
                    for m, (w, x) in enumerate(((wh, hi), (wh, lo), (wl, hi))):
                        ins = pe.matmul(dst, w, x[:, kt, c0:c1], start=first and n == 0 and m == 0,
                                        stop=last and n == len(kts) - 1 and m == 2)
                ins.then_inc(half_done if done else part_done, 1)

            def unit(b, j, qb, q, cols=(0, T), fresh=None):
                bank_wait(qb, q)
                dst = proj[q % 2][:, 0:cols[1] - cols[0]]
                f = None if fresh is None else (ht_ready, fresh)
                accumulate(b, j, dst, range(0, 8), 0, ht_hi, ht_lo, cols, True, False, f)
                accumulate(b, j + 1, dst, range(8, 16), 0, ht_hi, ht_lo, cols, False, True, f)

            def first_units(b, qb, q, fresh):
                bank_wait(qb, q)
                bank_wait(qb, q + 1)
                for kt in range(KT):
                    part, n = kt // 8, kt % 8
                    if n == 0:
                        pe.wait_ge(lo_done, th(b, 2 + part))
                    pe.wait_ge(ht_ready, fresh + kt + 1)
                    for u in range(2):
                        slot = 2 * u + part
                        wh, wl = [w[:, slot, n * P:(n + 1) * P] for w in (w_hi, w_lo)]
                        for m, (w, x) in enumerate(((wh, ht_hi), (wh, ht_lo), (wl, ht_hi))):
                            ins = pe.matmul(proj[(q + u) % 2][:], w, x[:, kt, :], start=kt == 0 and m == 0,
                                            stop=kt == KT - 1 and m == 2)
                            if (kt, u, m) in ((7, 0, 2), (15, 0, 2), (15, 1, 0), (15, 1, 2)):
                                ins.then_inc(half_done, 1)

            def taken(qb, q):
                pe.wait_ge(bank_free[q % 2], qb + q // 2 + 1)

            def transposes(dst, srcs):
                for n, src in enumerate(srcs):
                    k, m = src.shape
                    ins = pe.transpose(dst[0:m, n * P:n * P + k], src, ident[0:k, 0:k])
                return ins

            def blocks(tile, n=NT):
                return [tile[:, t * P:(t + 1) * P] for t in range(n)]

            pe.wait_ge(consts_built, CONSTS)
            pe.wait_ge(params_in, 16 * NPAR_DMA)
            at_col = 0
            for s in range(3):
                n = sum(x[1] for x in STACKS[s])
                ins = pe.transpose(TB[0][:, at_col:at_col + n], stack[s][0:n, :], ident[0:n, 0:n])
                at_col += n
            ins.then_inc(pro_pe.sem, 1)
            pe.wait_ge(mem_scaled, 4)
            for k in range(KT):
                if k >= 4:
                    pe.wait_ge(ht_ready, HT_MEM + k - 3)
                transposes(S[k % 4], [mem_tok[:, t, k * P:(k + 1) * P] for t in range(4)]).then_inc(memt_pe, 1)
            pe.wait_ge(x_in, 16)
            for k in range(KT):
                if k < 4:
                    pe.wait_ge(ht_ready, HT_MEM + 13 + k)
                else:
                    pe.wait_ge(xt_x, k - 3)
                transposes(S[k % 4], [x_tok[:, t, k * P:(k + 1) * P] for t in range(NT)]).then_inc(xt_pe, 1)

            def kv(b, qb, src, fresh, n):
                cols = (src * M, src * M + M)
                unit(b, 0, qb, 0, cols, fresh)
                unit(b, 2, qb, 1, cols)
                taken(qb, 1)
                need(pe, v1_done, n)
                transposes(TB[0], blocks(kv_v, 2)).then_inc(kv_t, 1)


            def norm_sums(count, acc, dst=TB[1]):
                pe.wait_ge(norm_acc, count)
                pe.matmul(dst[:], ones[:], acc[:], start=True, stop=True).then_inc(norm_sum, 1)

            kv(0, 0, 0, HT_MEM, 0)
            norm_sums(Z_X + KT, p_acc)
            with pe.Fori(1, 4) as i:
                kv(i, i, 0, None, i)
            with pe.Fori(0, 4) as i:
                kv(i + 4, i + 4, 1, None, i + 4)

            def lru_iter(b, qb, i, fresh=None):
                if fresh is None:
                    unit(b, 0, qb, 0)
                    unit(b, 2, qb, 1)
                else:
                    first_units(b, qb, 0, fresh)
                wait(pe, lru_dve, "xc", i)
                pe.matmul(S[0][:], l_w[:, 0, :], l_xc[:], start=True, stop=True)
                pe.matmul(S[1][:], l_w[:, 1, :], l_xc[:], start=True, stop=True).then_inc(lru_pe.sem, 1)

            lru_iter(H4["lru"], Q2["lru"], 0, HT_X)
            with pe.Fori(1, LRU_BLOCKS) as i:
                lru_iter(i + H4["lru"], i + Q2["lru"], i)

            hb, qb = H4["mlg"], Q2["ml"]
            for q in range(4):
                accumulate(hb, q, S[3][:], range(4 * q, 4 * q + 4), 0, ht_hi, ht_lo, (0, T), q == 0, q == 3)

            def ml_out(pr):
                wait(pe, ml_dve, "hn", pr)
                for x in range(3):
                    transposes(S[x], [m_hr[:, c, x * P:(x + 1) * P] for c in range(NT)]).then_inc(ml_pe.sem, 1)

            for pr in range(ML_PAIRS):
                def signal(ins, name):
                    assert ml_pe.names.index(name) == order[0], name
                    order[0] += 1
                    ins.then_inc(ml_pe.sem, 1)

                order = [0]
                h0, q0 = 18 * pr, 9 * pr

                def ml_unit(u):
                    unit(H4["ml"], h0 + 2 * u, qb, q0 + u)

                def ml_qkv(x):
                    wait(pe, ml_dve, f"uc{x}", pr)
                    if x == 1:
                        wait(pe, ml_act, "q0", pr)
                    if x == 2:
                        wait(pe, ml_act, "q1", pr)
                    if x:
                        wait(pe, ml_dve, f"v{x - 1}", pr)
                    for m, src in enumerate((m_uc[:], m_uc[:], m_up[:, 3:3 + T])):
                        ins = pe.matmul(S[m][:], m_bd[:, m, x, :], src, start=True, stop=True)
                    signal(ins, f"qk{x}")

                def ml_v(x):
                    wait(pe, ml_dve, f"v{x}", pr)
                    if x:
                        wait(pe, ml_act, f"vt{x - 1}", pr)
                    signal(transposes(TB[0], blocks(m_hf[:, x * T:(x + 1) * T])), f"v{x}")

                def ml_o(x):
                    wait(pe, ml_act, f"o{x}", pr)
                    wait(pe, ml_act, "vt2", pr)
                    if x:
                        wait(pe, ml_dve, f"ot{x - 1}", pr)
                    signal(transposes(TB[0], blocks((m_uc, m_up, m_uc)[x][:, 3 * (x % 2):3 * (x % 2) + T])), f"o{x}")

                def ml_scores(c):
                    cc = slice(c * P, (c + 1) * P)
                    if c:
                        wait(pe, ml_dve, f"se{c - 1}", pr)
                    else:
                        wait(pe, ml_dve, "k2", pr)
                        wait(pe, ml_act, "gc", pr)
                        wait(pe, ml_act, "q2", pr)
                    for hh in range(2):
                        d = slice(hh * P, (hh + 1) * P)
                        pe.matmul(S[0][:, d], m_k[:, 2 * hh, cc], m_q[:, 3 * hh, cc], start=True, stop=False)
                        pe.matmul(S[0][:, d], m_k[:, 1, cc], m_q[:, 1 + hh, cc], start=False, stop=True)
                        pe.matmul(S[1][:, d], sel[:, hh, :], r_r[0:2, cc], start=True, stop=False)
                        ins = pe.matmul(S[1][:, d], ident[:], m_neg[:], start=False, stop=True)
                    signal(ins, f"st{c}")

                def ml_core(c):
                    cc = slice(c * P, (c + 1) * P)
                    if c < NT - 1:
                        if c:
                            wait(pe, ml_dve, f"c{c - 1}", pr)
                        else:
                            wait(pe, ml_dve, "ot2", pr)
                        signal(transposes(TB[0], [m_k[:, x, cc] for x in range(3)]), f"kt{c}")
                    wait(pe, ml_dve, f"se{c}", pr)
                    if c:
                        wait(pe, ml_dve, f"c{c - 1}", pr)
                        wait(pe, ml_act, f"tot{c - 1}", pr)
                    for hh in range(2):
                        d = slice(hh * 256, hh * 256 + ML_DH + 1)
                        ins = pe.matmul(S[2][:, d], m_e[:, hh, :], m_v[:, c, hh, :], start=True, stop=True)
                        if c:
                            pe.matmul(S[3][:, d], m_q[:, 3 * hh, cc], m_c[:, 2 * hh, :], start=True, stop=False)
                            ins = pe.matmul(S[3][:, d], m_q[:, 1 + hh, cc], m_c[:, 1, :], start=False, stop=True)
                    signal(ins, f"num{c}")
                    if c < NT - 1:
                        wait(pe, ml_act, f"kts{c}", pr)
                        n = ML_DH + 1
                        pe.matmul(TB[1][:, 0:n], m_kt[:, 0, 0:P], m_v[:, c, 0, :], start=True, stop=True)
                        pe.matmul(TB[1][0:64, 256:256 + n], m_kt[:, 0, P:ML_DH], m_v[:, c, 0, :], start=True, stop=True)
                        pe.matmul(TB[1][64:P, 256:256 + n], m_kt[:, 1, 0:64], m_v[:, c, 1, :], start=True, stop=True)
                        signal(pe.matmul(TB[0][:, 0:n], m_kt[:, 1, 64:ML_DH], m_v[:, c, 1, :], start=True, stop=True),
                               f"cu{c}")

                ml_unit(0)
                if pr:
                    ml_out(pr - 1)
                wait(pe, ml_gate, "rows")
                if pr:
                    wait(pe, ml_dve, "y", pr - 1)
                pe.matmul(S[0][0:2, :], ident[0:8, 2 * pr:2 * pr + 2], gate_rows[0:8, :], start=True, stop=True)
                signal(pe.matmul(S[1][0:2, :], ident[0:8, 4 + 2 * pr:6 + 2 * pr], gate_rows[0:8, :],
                                 start=True, stop=True), "gates")
                ml_unit(1)
                wait(pe, ml_act, "ln", pr)
                ml_qkv(0)
                ml_unit(2)
                ml_v(0)
                ml_qkv(1)
                ml_unit(3)
                wait(pe, ml_act, "rows", pr)
                signal(transposes(TB[1], blocks(m_g)), "g")
                for hh in range(2):
                    ins = pe.matmul(S[3][:, 4 * hh:4 * hh + 4], sel[:, hh, :], m_sm[0:2, 12:16], start=True, stop=True)
                signal(ins, "sold")
                ml_v(1)
                ml_qkv(2)
                ml_unit(4)
                ml_v(2)
                ml_unit(5)
                ml_o(0)
                ml_o(1)
                ml_unit(6)
                ml_o(2)
                ml_scores(0)
                ml_unit(7)
                ml_core(0)
                ml_scores(1)
                ml_unit(8)
                ml_core(1)
                for c in (2, 3):
                    ml_scores(c)
                    ml_core(c)

            def scores(n, q, k, geo, k0=None, all_taken=None):
                pe.wait_ge(att_ok, n + 1)
                for t, (b0, nb) in enumerate(geo):
                    if k0 is not None and t < NT - 1:
                        pe.wait_ge(att_k, k0 + t + 1)
                    elif k0 is not None:
                        all_taken()
                    pe.matmul(S[t][:, 0:nb * P], q[:, t * P:(t + 1) * P], k[:, b0 * P:(b0 + nb) * P],
                              start=True, stop=True).then_inc(att_s, 1)

            def values(n, l, pt, v, geo):
                offs = [sum(g[1] for g in geo[:t]) * P for t in range(NT)]

                def product(t):
                    b0, nb = geo[t]
                    pe.wait_ge(att_c, n * 4 + t + 1)
                    for x in range(nb):
                        ins = pe.matmul(S[0][:, t * P:(t + 1) * P], pt[:, offs[t] + x * P:offs[t] + (x + 1) * P],
                                        v(b0 + x), start=x == 0, stop=x == nb - 1)
                    return ins

                for t, (b0, nb) in enumerate(geo):
                    pe.wait_ge(att_e, n * 4 + t + 1)
                    if t >= 2:
                        pe.wait_ge(att_c, n * 4 + t - 1)
                    transposes(TB[t % 2], [l[:, offs[t] + x * P:offs[t] + (x + 1) * P] for x in range(nb)]
                               ).then_inc(att_p, 1)
                    if t:
                        product(t - 1)
                product(NT - 1).then_inc(att_o, 1)

            def out_t(n, o):
                pe.wait_ge(att_ok, n + 2)
                transposes(TB[0], blocks(o)).then_inc(att_ot, 1)

            def v_t(y, v):
                pe.wait_ge(*y)
                transposes(TB[0], blocks(v)).then_inc(att_vt, 1)

            def tok(t):
                return lambda b: t[:, b * P:(b + 1) * P]

            def moba_head(b, qb, i, before):
                unit(b, 0, qb, 0)
                if before:
                    out_t(i - 1, a_o)
                else:
                    ml_out(ML_PAIRS - 1)
                unit(b, 2, qb, 1)
                taken(qb, 0)
                v_t((att_y, i + 1), a_v)
                unit(b, 4, qb, 2)
                taken(qb, 1)
                scores(i, a_q, a_k, CAUSAL, i * 3, lambda: taken(qb, 2))
                unit(b, 6, qb, 3)
                pe.wait_ge(att_vc, i + 1)
                values(i, a_l, a_pt, tok(a_vt), CAUSAL)

            moba_head(H4["moba"], Q2["moba"], 0, False)
            with pe.Fori(1, MO_HEADS) as i:
                moba_head(i * 2 + H4["moba"], i * 2 + Q2["moba"], i, True)
            out_t(MO_HEADS - 1, a_o)

            def wide(name, fresh):
                unit(H4[name], 0, Q2[name], 0, fresh=fresh)
                unit(H4[name], 2, Q2[name], 1)
                with pe.Fori(1, KT // 2) as i:
                    unit(i + H4[name], 0, i + Q2[name], 0)
                    unit(i + H4[name], 2, i + Q2[name], 1)

            wide("wout", HT_Y)
            norm_sums(Z_X1 + KT, n_acc)
            for h in range(XA_HEADS + 1):
                if h == 0:
                    first_units(H4["xq"], Q2["xq"], 0, HT_X1)
                elif 1 < h < XA_HEADS:
                    unit(H4["xq"], 2 * h, Q2["xq"], h)
                if h:
                    n = A_XA + h - 1
                    if h == 1:
                        pe.wait_ge(att_y, MO_HEADS + 1)
                    else:
                        pe.wait_ge(yh_f, h - 1)
                    values(n, b_l, b_pt, lambda blk, h=h: v1[:, h - 1, blk, :], FULL)
                    out_t(n, b_o)
                if h < XA_HEADS:
                    taken(Q2["xq"], h)
                    scores(A_XA + h, b_q, k1[:, h, :], FULL)

            def xwo(b, qb, fresh):
                for q in range(8):
                    bank_wait(qb, q)
                    accumulate(b, q // 2, proj[q % 2][:], range(4), q % 2, o_hi, o_lo, (0, T), True, True,
                               (yh_ready, YH_XA) if fresh and q == 0 else None, done=q % 2 == 1, step=2)

            xwo(H4["xwo"], Q2["xwo"], True)
            xwo(H4["xwo"] + 1, Q2["xwo"] + 4, False)
            norm_sums(Z_X2 + 2 * KT, n_acc)
            norm_sums(Z_X2 + 2 * KT, n_acc3, TB[0])

            for q in range(4):
                accumulate(H4["glr"], q, S[3][:], range(4 * q, 4 * q + 4), 0, ht_hi, ht_lo, (0, T), q == 0, q == 3,
                           (ht_ready, HT_H2))
            def gla_out(i):
                wait(pe, gla_dve, "o", i)
                for x in range(2):
                    ins = transposes(S[1 + x], [g_o[:, t, x * P:(x + 1) * P] for t in range(NT)])
                ins.then_inc(gla_pe.sem, 1)

            def gla_head(b, qb, i, before):
                unit(b, 0, qb, 0)
                if before:
                    gla_out(i - 1)
                pe.wait_ge(gla_wh, i + 1)
                pe.matmul(S[0][:], g_wh[:], g_lr[:], start=True, stop=True).then_inc(gla_pe.sem, 1)
                unit(b, 2, qb, 1)
                unit(b, 4, qb, 2)
                wait(pe, gla_dve, "kk", i)
                transposes(TB[0], blocks(g_kk)).then_inc(gla_pe.sem, 1)
                taken(qb, 2)
                transposes(TB[1], blocks(g_v)).then_inc(gla_pe.sem, 1)
                unit(b, 6, qb, 3)
                taken(qb, 3)
                wait(pe, gla_act, "kkt", i)
                transposes(TB[0], blocks(g_v)).then_inc(gla_pe.sem, 1)
                for p2 in range(4):
                    c = slice(p2 * P, (p2 + 1) * P)
                    ins = pe.matmul(S[0][:, c], g_kt[:, c], g_qt[:, c], start=True, stop=True)
                ins.then_inc(gla_pe.sem, 1)
                unit(b, 8, qb, 4)
                wait(pe, gla_dve, "vb", i)
                for c in range(7):
                    r = slice(64 * (c % 2), 64 * (c % 2) + 64)
                    ins = pe.matmul(gla_kv(c), g_kkt[r, c // 2, :], g_vt[r, c // 2, :], start=True, stop=True)
                ins.then_inc(gla_pe.sem, 1)
                unit(b, 10, qb, 5)
                wait(pe, gla_dve, "st", i)
                for p2 in range(4):
                    o = (S[0], TB[0])[p2 // 2]
                    c0 = (p2 % 2) * 256
                    pe.matmul(o[:, c0:c0 + 256], g_at[:, p2, :], g_vt[:, p2, :], start=True, stop=False,
                              skip_group_check=True)
                    for r in range(2):
                        c = 2 * p2 + r
                        if c:
                            ins = pe.matmul(o[64 * r:64 * r + 64, c0:c0 + 256],
                                            g_qt[:, c * 64:(c + 1) * 64], g_st[:, c - 1, :], start=False,
                                            stop=True, skip_group_check=True)
                ins.then_inc(gla_pe.sem, 1)

            gla_head(H4["gla"], Q2["gla"], 0, False)
            with pe.Fori(1, GLA_HEADS) as i:
                gla_head(i * 3 + H4["gla"], i * 3 + Q2["gla"], i, True)
            gla_out(GLA_HEADS - 1)

            def merge(name, yh0):
                with pe.Fori(0, 4) as i:
                    b, qb = i * 3 + H4[name], i * 4 + Q2[name]
                    for t in range(4):
                        unit(b, 3 * t, qb, 2 * t)
                        if t == 0:
                            pe.wait_ge(yh_ready, yh0 + 8)
                        bank_wait(qb, 2 * t + 1)
                        accumulate(b, 3 * t + 2, proj[1][:], range(8), 0, yh, yl, (0, T), True, True)

            merge("merge_g", YH_GLA)

            def swa_out(i):
                wait(pe, comb_dve, "m", i)
                transposes(TB[0], blocks(w_og[:, 0, :])).then_inc(att_ot, 1)

            def swa_head(b, qb, i, before):
                for g in range(SWA_GROUPS + 1):
                    n = i * 3 + A_SWA + g
                    geo = (WINDOW, CAUSAL, CAUSAL)[g % 3]
                    unit(b, 6 * g, qb, 3 * g)
                    if before and g == 0:
                        swa_out(i - 1)
                    if g:
                        pe.wait_ge(att_vc, i * 3 + MO_HEADS + g)
                        values(n - 1, w_l, w_pt, tok(w_vt), (WINDOW, CAUSAL, CAUSAL)[g - 1])
                    if g == SWA_GROUPS:
                        break
                    unit(b, 6 * g + 2, qb, 3 * g + 1)
                    taken(qb, 3 * g)
                    v_t((yh_f, i + 4), w_v)
                    unit(b, 6 * g + 4, qb, 3 * g + 2)
                    taken(qb, 3 * g + 1)
                    scores(n, w_q, w_k, geo, i * 9 + 3 * (MO_HEADS + g), lambda: taken(qb, 3 * g + 2))

            swa_head(H4["swa"], Q2["swa"], 0, False)
            with pe.Fori(1, SWA_HPG) as i:
                swa_head(i * 5 + H4["swa"], i * 5 + Q2["swa"], i, True)

            def mem_head(b, qb, i, before):
                unit(b, 0, qb, 0)
                if before:
                    out_t(i - 1 + A_MEM, c_o)
                else:
                    swa_out(SWA_HPG - 1)
                taken(qb, 0)
                scores(i + A_MEM, c_q, k2[:, i, :], FULL)
                unit(b, 2, qb, 1)
                pe.wait_ge(yh_f, i + 8)
                values(i + A_MEM, c_l, c_pt, lambda blk: v2[:, i, blk, :], FULL)

            mem_head(H4["mem"], Q2["mem"], 0, False)
            with pe.Fori(1, MEM_HEADS) as i:
                mem_head(i + H4["mem"], i + Q2["mem"], i, True)
            out_t(MEM_HEADS - 1 + A_MEM, c_o)

            with pe.Fori(0, 4) as i:
                b, qb = i * 5 + H4["merge_sm"], i * 8 + Q2["merge_sm"]
                for t in range(4):
                    unit(b, 5 * t, qb, 4 * t)
                    unit(b, 5 * t + 2, qb, 4 * t + 1)
                    if t == 0:
                        pe.wait_ge(yh_ready, YH_MEM + 4)
                    for x in range(2):
                        bank_wait(qb, 4 * t + 2 + x)
                        accumulate(b, 5 * t + 4, proj[x][:], range(4 * x, 4 * x + 4), 4 * x, yh, yl, (0, T),
                                   True, True, done=x == 1)

            for g in range(POOL_GROUPS):
                for u in range(3):
                    unit(H4["pool"], 8 * g + 2 * u, Q2["pool"], 4 * g + u)
                wait(pe, pool_dve, "p", g)
                if g:
                    wait(pe, pool_dve, "y1", g - 1)
                else:
                    pe.wait_ge(weights_in, 16 * 7)
                for d in range(2):
                    for c in range(2):
                        ins = pe.matmul(S[d][:], p_w[:, g, c, d, :], p_p[c][:], start=c == 0, stop=c == 1)
                ins.then_inc(pool_pe.sem, 1)
                unit(H4["pool"], 8 * g + 6, Q2["pool"], 4 * g + 3)
            merge("merge_p", YH_POOL)

            wide("wout2", HT_MERGED)
            norm_sums(Z_Y2 + KT, f_acc)
            for k in range(KT):
                pe.wait_ge(fin_dve, k + 1)
                if k >= 4:
                    pe.wait_ge(fin_copy, k - 3)
                transposes(S[k % 4], blocks(xy[:, k, :])).then_inc(fin_pe, 1)

        @block.scalar
        def _(act):
            link = Chain(act, act_chain)
            last_half = NH

            def ahead(b, j, halves=2, extra=None):
                for d in range(halves):
                    jj = j + d + 2
                    if isinstance(b, int) and 4 * b + jj >= last_half:
                        return
                    slot = jj % RING
                    act.wait_ge(raw_ready[slot], 16 * (b + jj // RING) + 16)
                    if extra is not None and extra[0] == d:
                        act.wait_ge(mem_half_ready, extra[1])
                    need(act, half_done, th(b, jj) - RING)
                    act.activation(w_hi[:, slot, :], raw[:, slot, :], ACT.Copy).then_inc(hi_done, 1)

            def unit_in(b, j):
                act.wait_ge(half_done, th(b, j))

            phase = [0]

            def phase_end():
                phase[0] += 1
                act.wait_ge(act_chain, link.base + link.n)
                act.sem_inc(act_phase, 1)
                act.wait_ge(dve_phase, phase[0])

            act.wait_ge(consts_built, CONSTS)
            for t in range(4):
                act.wait_ge(mem_in[t], 16)
                link(act.activation(unread[t % 2][:], mem_tok[:, t, :], ACT.Square, accum_out=mem_ss[:, t:t + 1]))
            act.activation(mem_rstd, mem_ss, ACT.Sqrt, scale=1.0 / D, bias=eps_rms).then_inc(pro_act.sem, 2)
            wait(act, pro_dve, "rstd")
            for t in (2, 3):
                act.activation(mem_tok[:, t, :], mem_tok[:, t, :], ACT.Copy, scale=mem_rstd[:, t:t + 1]
                               ).then_inc(mem_scaled, 1)
            for h in range(2):
                act.wait_ge(raw_ready[h], 16)
                act.activation(w_hi[:, h, :], raw[:, h, :], ACT.Copy).then_inc(hi_done, 1)
            wait(act, pro_dve, "params")
            for k in range(KT):
                act.wait_ge(memt_pe, k + 1)
                link.inc(act.activation(ht_hi[:, k, 0:M], S[k % 4][:, 0:M], ACT.Copy, scale=col("mem_norm_g", k)))
                act.activation(ht_hi[:, k, M:T], S[k % 4][:, M:T], ACT.Copy, scale=col("g_mem", k)).then_inc(memt_hi, 1)

            def squares(src, dst, n, gain=1.0, added=None):
                need(act, norm_acc, n if added is None else added)
                act.activation(dst, src, ACT.Square, scale=gain).then_inc(norm_sq, 1)

            def root(n):
                act.wait_ge(norm_sum, n)
                act.activation(nt["rstd"][:], TB[1][:], ACT.Sqrt, scale=1.0 / D, bias=eps_rms).then_inc(norm_root, 1)

            def kv(b, qb, i, ks):
                ahead(b, 0)
                unit_in(b, 1)
                act.activation((k1, k2)[ks][:, i, :], proj[0][:, 0:M], ACT.Copy).then_inc(bank_free[0], 1)
                ahead(b, 2)

            ahead(0, 0)
            for k in range(KT):
                act.wait_ge(xt_x, k + 1)
                squares(x_t[:, k, :], p_sq[:], Z_X + k)
            unit_in(0, 1)
            act.activation(k1[:, 0, :], proj[0][:, 0:M], ACT.Copy).then_inc(bank_free[0], 1)
            ahead(0, 2)
            nt = {"rstd": n0[0], "t": n0[1:3]}
            root(1)
            with act.Fori(1, 4) as i:
                kv(i, i, i, 0)
            with act.Fori(0, 4) as i:
                kv(i + 4, i + 4, i, 1)

            def highs(done, base):
                act.wait_ge(half_done, done)
                for k in range(KT):
                    act.wait_ge(norm_t, base + k + 1)
                    act.activation(ht_hi[:, k, :], nt["t"][k % 2][:], ACT.Copy).then_inc(norm_hi, 1)

            lam = par[:, PARAM["lru_lambda"]:PARAM["lru_lambda"] + 4]
            link(act.activation(lru_half_c, lam, ACT.Abs))
            link(act.activation(lru_half_c, lru_half_c, ACT.Exp, scale=-1.0))
            act.activation(lru_half_c, lru_half_c, ACT.Ln, bias=ones[:, 0:1]).then_inc(lru_lam, 1)
            ahead(H4["lru"], 0)
            highs(4 * H4["lru"], 0)
            act.wait_ge(spilled, 16)
            phase_end()

            act.wait_ge(lru_c, 1)

            def lru_iter(b, qb, i):
                unit_in(b, 1)
                if not isinstance(i, int):
                    wait(act, lru_dve, "xc", i - 1)
                    wait(act, lru_pe, "gates", i - 1)
                act.activation(l_xp[:, 3:3 + T], proj[0][:], ACT.Copy).then_inc(bank_free[0], 1)
                ahead(b, 2)
                ahead(b, 4)
                wait(act, lru_pe, "gates", i)
                link(act.activation(l_tr[:], S[0][:], ACT.Tanh, scale=0.5, bias=lru_hba[:, bass.ds(i, 1)]))
                act.activation(l_ti[:], S[1][:], ACT.Tanh, scale=0.5, bias=lru_hbx[:, bass.ds(i, 1)]).then_inc(lru_act.sem, 1)
                c = lru_half_c[:, bass.ds(i, 1)]
                act.activation(l_t[:], l_tr[:], ACT.Tanh, scale=c, bias=c).then_inc(lru_act.sem, 1)
                act.activation(l_tz[:], proj[1][:], ACT.Tanh, scale=0.5).then_inc(lru_act.sem, 1)
                wait(act, lru_dve, "s", i)
                act.activation(l_h[:], l_s[:], ACT.Sqrt, scale=-1.0).then_inc(lru_act.sem, 1)

            lru_iter(H4["lru"], Q2["lru"], 0)
            with act.Fori(1, LRU_BLOCKS) as i:
                link.enter(i - 1, 1)
                lru_iter(i + H4["lru"], i + Q2["lru"], i)
            link.leave(3)
            ahead(H4["mlg"], 2)
            phase_end()
            for m, name in enumerate(("ml_wq", "ml_wk", "ml_wv")):
                act.dma_start(m_wd[:, m, :, :], a[name][0].rearrange("g i o -> (g i) o").rearrange(
                    "(x p) o -> p x o", p=P)).then_inc(weights_in, 16)

            hb, qb = H4["ml"], Q2["ml"]
            for pr in range(ML_PAIRS):
                order = [0]

                def signal(ins, name):
                    assert ml_act.names.index(name) == order[0], name
                    order[0] += 1
                    ins.then_inc(ml_act.sem, 1)

                h0, q0 = 18 * pr, 9 * pr

                def ml_ahead(u):
                    ahead(hb, h0 + 2 * u)

                def ml_in(u):
                    unit_in(hb, h0 + 2 * u + 1)
                    return proj[(q0 + u) % 2], bank_free[(q0 + u) % 2]

                def ml_u(x):
                    src, free = ml_in(x)
                    if x:
                        wait(act, ml_pe, f"qk{x - 1}", pr)
                        wait(act, ml_dve, f"uc{x - 1}", pr)
                    act.activation(m_up[:, 3:3 + T], src[:], ACT.Copy).then_inc(free, 1)

                def ml_th(x):
                    act.wait_ge(ml_conv, 3 * pr + x + 1)
                    signal(act.activation(m_hf[:, x * T:(x + 1) * T], m_uc[:], ACT.Tanh, scale=0.5), f"th{x}")

                def ml_qv(x):
                    wait(act, ml_pe, f"qk{x}", pr)
                    if x == 1:
                        link.inc(act.activation(m_q[0:64, 1, :], S[0][0:64, :], ACT.Copy, scale=0.5))
                        ins = act.activation(m_q[64:P, 2, :], S[0][64:P, :], ACT.Copy, scale=0.5)
                    else:
                        ins = act.activation(m_q[:, 3 * x // 2, :], S[0][:], ACT.Copy, scale=0.5)
                    signal(ins, f"q{x}")

                def ml_vt(x):
                    wait(act, ml_pe, f"v{x}", pr)
                    t0 = TB[0][:].rearrange("p (c n) -> p c n", n=P)
                    if x == 0:
                        ins = act.activation(m_v[:, :, 0, 0:P], t0, ACT.Copy)
                    elif x == 1:
                        link.inc(act.activation(m_v[:, :, 0, P:ML_DH], t0[:, :, 0:64], ACT.Copy))
                        ins = act.activation(m_v[:, :, 1, 0:64], t0[:, :, 64:P], ACT.Copy)
                    else:
                        ins = act.activation(m_v[:, :, 1, 64:ML_DH], t0, ACT.Copy)
                    signal(ins, f"vt{x}")

                def ml_oz(x):
                    src, free = ml_in(3 + x)
                    wait(act, ml_pe, "qk2", pr)
                    if x == 2:
                        wait(act, ml_pe, "o0", pr)
                    signal(act.activation((m_uc, m_up, m_uc)[x][:, 3 * (x % 2):3 * (x % 2) + T], src[:], ACT.Tanh, scale=0.5), f"o{x}")
                    act.wait_ge(ml_act.sem, ml_act.value(f"o{x}", pr))
                    act.sem_inc(free, 1)

                def ml_z(x):
                    src, free = ml_in(6 + x)
                    signal(act.activation(xy[:, 4 + 3 * pr + x, :], src[:], ACT.Tanh, scale=0.5), f"z{x}")

                def ml_exp(c):
                    wait(act, ml_pe, f"st{c}", pr)
                    if c:
                        wait(act, ml_dve, f"se{c - 1}", pr)
                    for hh in range(2):
                        ins = act.activation(m_e[:, hh, :], S[1][:, hh * P:(hh + 1) * P], ACT.Exp,
                                             bias=m_gc[:, c, hh:hh + 1])
                        if hh == 0:
                            link.inc(ins)
                    signal(ins, f"e{c}")

                def ml_core(c):
                    if c < NT - 1:
                        wait(act, ml_pe, f"kt{c}", pr)
                        for hh in range(2):
                            ins = act.activation(m_kt[:, hh, :], TB[0][:, hh * ML_DH:(hh + 1) * ML_DH], ACT.Copy,
                                                 scale=m_gc[:, c, 96 + hh:97 + hh])
                            if hh == 0:
                                link.inc(ins)
                        signal(ins, f"kts{c}")
                    wait(act, ml_pe, f"num{c}", pr)
                    for hh in range(2):
                        n = slice(hh * 256, hh * 256 + ML_DH + 1)
                        if c:
                            ins = act.activation(m_tot[:, hh, :], S[3][:, n], ACT.Copy, scale=m_gc[:, c, 32 + hh:33 + hh])
                        else:
                            ins = act.activation(m_tot[:, hh, :], S[2][:, n], ACT.Copy)
                        if hh == 0:
                            link.inc(ins)
                    signal(ins, f"tot{c}")

                ml_ahead(0)
                ml_ahead(1)
                ml_u(0)
                wait(act, ml_pe, "gates", pr)
                if pr:
                    wait(act, ml_dve, "hn", pr - 1)
                link(act.activation(r_ig[0:2, :], S[0][0:2, :], ACT.Identity, bias=gate_bias[:, pr:pr + 1]))
                link(act.activation(r_f[0:2, :], S[1][0:2, :], ACT.Identity, bias=gate_bias[:, 2 + pr:3 + pr]))
                link(act.activation(r_b[0:2, :], r_f[0:2, :], ACT.Abs))
                link(act.activation(r_b[0:2, :], r_b[0:2, :], ACT.Exp, scale=-1.0))
                signal(act.activation(r_b[0:2, :], r_b[0:2, :], ACT.Ln, bias=ones[0:2, 0:1]), "ln")
                ml_th(0)
                ml_ahead(2)
                ml_qv(0)
                ml_u(1)
                wait(act, ml_dve, "rows", pr)
                for c in range(NT):
                    cc = slice(c * P, (c + 1) * P)
                    link.inc(act.activation(m_g[32:34, cc], r_r[0:2, cc], ACT.Exp, bias=m_sm[0:2, c:c + 1]))
                    link.inc(act.activation(m_g[96:98, cc], m_g[0:2, cc], ACT.Exp,
                                            bias=r_r[0:2, c * P + P - 1:c * P + P]))
                link.inc(act.activation(m_g[64:66, :], r_ig[0:2, :], ACT.Exp))
                signal(act.activation(m_sm[0:2, 12:16], m_sm[0:2, 8:12], ACT.Exp), "rows")
                ml_th(1)
                ml_ahead(3)
                ml_vt(0)
                ml_qv(1)
                ml_u(2)
                ml_th(2)
                ml_ahead(4)
                wait(act, ml_pe, "g", pr)
                signal(act.activation(m_gc[:], TB[1][:].rearrange("p (c n) -> p c n", n=P), ACT.Copy), "gc")
                ml_vt(1)
                ml_qv(2)
                ml_oz(0)
                ml_ahead(5)
                ml_vt(2)
                ml_oz(1)
                ml_ahead(6)
                ml_oz(2)
                ml_ahead(7)
                ml_exp(0)
                ml_z(0)
                ml_core(0)
                ml_ahead(8)
                ml_exp(1)
                ml_z(1)
                ml_z(2)
                ml_core(1)
                for c in (2, 3):
                    ml_exp(c)
                    ml_core(c)
                act.wait_ge(ml_var, pr + 1)
                signal(act.activation(m_sm[:, 24:32], m_mv[:, :, 1], ACT.Sqrt, bias=eps_ln), "root")
            phase_end()

            def exps(n, st, l, geo, masked):
                offs = [sum(g[1] for g in geo[:t]) * P for t in range(NT)]
                for t, (b0, nb) in enumerate(geo):
                    act.wait_ge(att_l, n * 4 + t + 1)
                    lt = l[:, offs[t]:offs[t] + nb * P]
                    act.activation(lt, lt if masked else S[t][:, 0:nb * P], ACT.Exp, bias=st[:, t:t + 1],
                                   accum_out=st[:, 4 + t:5 + t]).then_inc(att_e, 1)

            def copies(n, pt, geo):
                offs = [sum(g[1] for g in geo[:t]) * P for t in range(NT)]
                for t, (b0, nb) in enumerate(geo):
                    act.wait_ge(att_p, n * 4 + t + 1)
                    act.activation(pt[:, offs[t]:offs[t] + nb * P], TB[t % 2][:, 0:nb * P], ACT.Copy).then_inc(att_c, 1)

            with act.Fori(0, MO_HEADS) as i:
                b = i * 2 + H4["moba"]
                ahead(b, 0)
                unit_in(b, 1)
                act.activation(a_v[:], proj[0][:], ACT.Copy).then_inc(bank_free[0], 1)
                ahead(b, 2)
                unit_in(b, 3)
                act.activation(a_q[:], proj[1][:], ACT.Copy, scale=HEAD_SCALE).then_inc(bank_free[1], 1)
                act.wait_ge(att_vt, i + 1)
                act.wait_ge(att_ok, i + 1)
                act.activation(a_vt[:], TB[0][:], ACT.Copy).then_inc(att_vc, 1)
                ahead(b, 4)
                exps(i, a_st, a_l, CAUSAL, True)
                ahead(b, 6)
                unit_in(b, 7)
                act.wait_ge(att_y, i + 1)
                act.activation(a_z[:], proj[1][:], ACT.Tanh, scale=0.5).then_inc(moz_act.sem, 1)
                copies(i, a_pt, CAUSAL)

            act.wait_ge(half_done, 4 * H4["wout"])
            act.wait_ge(att_y, MO_HEADS + 1)
            for k in range(KT):
                act.activation(ht_hi[:, k, :], xy[:, k, :], ACT.Copy).then_inc(norm_hi, 1)
            phase_end()

            for u in range(2):
                act.dma_start(n_x[u][:], x_spill[u]).then_inc(tile_in[u], 16)

            def wout_iter(b, qb, i, x_back):
                for u in range(2):
                    ahead(b, 2 * u)
                    n = i * 2 + u
                    act.wait_ge(bank_free[u], qb + 1)
                    if x_back:
                        act.dma_start(n_x[u][:], x_spill[n + 2]).then_inc(tile_in[u], 16)
                    squares(xy[:, n, :], n_sq[:], n + Z_X1)

            with act.Fori(0, KT // 2 - 1) as i:
                wout_iter(i + H4["wout"], i + Q2["wout"], i, True)
            wout_iter(KT // 2 - 1 + H4["wout"], KT // 2 - 1 + Q2["wout"], KT // 2 - 1, False)
            nt = {"rstd": n_rstd, "t": [n_t0, n_t1]}
            root(2)
            ahead(H4["xq"], 0)
            highs(4 * H4["xq"], KT)

            for h in range(XA_HEADS + 1):
                if h < XA_HEADS:
                    if h:
                        ahead(H4["xq"], 2 * h)
                    unit_in(H4["xq"], 2 * h + 1)
                    act.wait_ge(att_s, 4 * (A_XA + h))
                    act.activation(b_q[:], proj[h % 2][:], ACT.Copy, scale=HEAD_SCALE).then_inc(bank_free[h % 2], 1)
                if h:
                    copies(A_XA + h - 1, b_pt, FULL)
                    act.wait_ge(yh_f, h)
                    act.activation(o_hi[:, h - 1, :], n_t0[:], ACT.Copy).then_inc(yh_hi, 1)
                if h < XA_HEADS:
                    exps(A_XA + h, b_st, b_l, FULL, False)

            with act.Fori(0, 2) as i:
                for q in range(8):
                    if q % 2 == 0:
                        ahead(i + H4["xwo"], q // 2, 1)
                    n = i * 8 + q
                    act.wait_ge(bank_free[q % 2], i * 4 + Q2["xwo"] + q // 2 + 1)
                    m = i * 16 + 2 * q + Z_X2
                    squares(xy[:, n, :], n_sq[:], m)
                    squares(xy[:, n, :], n_sq3[:], m + 1, par[:, bass.ds(n + PARAM["final_norm_g"], 1)], m)
            ahead(H4["glr"], 0)
            act.wait_ge(norm_v, 1)
            act.activation(n_rstd[:], n_rstd[:], ACT.Sqrt, scale=1.0 / D).then_inc(norm_root, 1)
            act.activation(n_rs[:], n_rs[:], ACT.Sqrt).then_inc(norm_root, 1)
            act.wait_ge(norm_root, 4)
            act.dma_start(root_spill, n_rs[:]).then_inc(spilled, 16)
            highs(4 * H4["glr"], 2 * KT)
            ahead(H4["glr"], 2)
            act.wait_ge(spilled, 48)
            phase_end()
            phase_end()
            act.dma_start(g_wal[:], a["w_alpha_2"][0]).then_inc(weights_in, 16)

            def gla_highs(i):
                for x in range(2):
                    wait(act, gla_dve, f"y{x}", i)
                    act.activation(yh[:, bass.ds(i * 2 + x, 1), :], g_y[:].rearrange("p (a n) -> p a n", a=1),
                                   ACT.Copy).then_inc(gla_act.sem, 1)

            def gla_head(b, i, before):
                ahead(b, 0)
                if before:
                    gla_highs(i - 1)
                wait(act, gla_pe, "z", i)
                link(act.activation(g_x[:], S[0][:], ACT.Identity, bias=par[:, bass.ds(i + PARAM["b_alpha"], 1)]))
                link(act.activation(g_e[:], g_x[:], ACT.Abs))
                link(act.activation(g_e[:], g_e[:], ACT.Exp, scale=-1.0))
                act.activation(g_e[:], g_e[:], ACT.Ln, bias=ones[:, 0:1]).then_inc(gla_act.sem, 1)
                ahead(b, 2)
                wait(act, gla_dve, "bc", i)
                link.inc(act.activation(g_e[:], g_b[:], ACT.Exp, scale=1.0 / 16))
                link.inc(act.activation(g_y[:], g_b[:], ACT.Exp, scale=-1.0 / 16))
                link.inc(act.activation(g_x[:], g_x[:], ACT.Exp, scale=1.0 / 16))
                act.activation(g_dec[:], g_b[:].rearrange("p (c n) -> p c n", n=64)[:, :, 63], ACT.Exp,
                               scale=1.0 / 16).then_inc(gla_act.sem, 1)
                ahead(b, 4)
                unit_in(b, 5)
                act.activation(g_v[:], proj[0][:], ACT.Copy).then_inc(bank_free[0], 1)
                wait(act, gla_pe, "kk", i)
                act.activation(g_kkt[:], TB[0][:].rearrange("p (c n) -> p c n", n=P), ACT.Copy).then_inc(gla_act.sem, 1)
                ahead(b, 6)
                unit_in(b, 7)
                wait(act, gla_pe, "va", i)
                act.activation(g_v[:], proj[1][:], ACT.Copy).then_inc(bank_free[1], 1)
                for x in range(2):
                    ahead(b, 8 + 2 * x)
                    unit_in(b, 9 + 2 * x)
                    act.activation(g_z[:, x, :], proj[x][:], ACT.Tanh, scale=0.5).then_inc(gla_act.sem, 1)
                wait(act, gla_pe, "o", i)
                for p2 in range(4):
                    o = (S[0], TB[0])[p2 // 2][:, (p2 % 2) * 256:(p2 % 2) * 256 + 256]
                    ins = act.activation(g_e[:, 0:256], o, ACT.Square, accum_out=g_ss[:, p2:p2 + 1])
                    if p2 < 3:
                        link(ins)
                ins.then_inc(gla_act.sem, 1)
                wait(act, gla_act, "sq", i)
                act.activation(g_ss[:, 4:8], g_ss[:, 0:4], ACT.Sqrt, scale=1.0 / GLA_DV, bias=eps_rms).then_inc(gla_act.sem, 1)

            gla_head(H4["gla"], 0, False)
            with act.Fori(1, GLA_HEADS) as i:
                link.enter(i - 1, 9)
                gla_head(i * 3 + H4["gla"], i, True)
            link.leave(GLA_HEADS - 1)
            gla_highs(GLA_HEADS - 1)
            phase_end()

            def merge(name, branch):
                with act.Fori(0, 4) as i:
                    b, qb = i * 3 + H4[name], i * 4 + Q2[name]
                    for t in range(4):
                        ahead(b, 3 * t, 3)
                        unit_in(b, 3 * t + 1)
                        act.wait_ge(bank_free[1], qb + t)
                        act.activation(e_th[t % 2][:], proj[0][:], ACT.Tanh, scale=0.5,
                                       bias=par[:, bass.ds(i * 4 + PARAM["b_merge"] + branch * KT + t, 1)]
                                       ).then_inc(bank_free[0], 1)

            merge("merge_g", 2)
            phase_end()

            def swa_high(i):
                act.wait_ge(yh_f, i + 5)
                act.activation(yh[:, bass.ds(i, 1), :], w_q[:].rearrange("p (a n) -> p a n", a=1), ACT.Copy
                               ).then_inc(yh_hi, 1)

            def swa_head(b, i, before):
                for g in range(SWA_GROUPS + 1):
                    n = i * 3 + A_SWA + g
                    geo = (WINDOW, CAUSAL, CAUSAL)
                    u = 3 * g
                    ahead(b, 6 * g)
                    unit_in(b, 6 * g + 1)
                    if g:
                        copies(n - 1, w_pt, geo[g - 1])
                    if g == SWA_GROUPS:
                        break
                    if g == 0:
                        if before:
                            swa_high(i - 1)
                        act.wait_ge(yh_ready, i + YH_SWA)
                    act.activation(w_v[:], proj[u % 2][:], ACT.Copy).then_inc(bank_free[u % 2], 1)
                    ahead(b, 6 * g + 2)
                    unit_in(b, 6 * g + 3)
                    act.activation(w_q[:], proj[(u + 1) % 2][:], ACT.Copy, scale=HEAD_SCALE).then_inc(bank_free[(u + 1) % 2], 1)
                    act.wait_ge(att_vt, i * 3 + MO_HEADS + g + 1)
                    act.wait_ge(att_ok, n + 1)
                    act.activation(w_vt[:], TB[0][:], ACT.Copy).then_inc(att_vc, 1)
                    ahead(b, 6 * g + 4)
                    exps(n, w_st[:, 12 * g:12 * g + 12], w_l, geo[g], True)
                act.activation(w_v[:], proj[1][:], ACT.Tanh, scale=0.5).then_inc(comb_act.sem, 1)
                act.wait_ge(comb_in, i + 1)
                act.activation(w_wt, w_wt, ACT.Exp).then_inc(comb_act.sem, 1)

            swa_head(H4["swa"], 0, False)
            with act.Fori(1, SWA_HPG) as i:
                swa_head(i * 5 + H4["swa"], i, True)
            swa_high(SWA_HPG - 1)
            phase_end()

            def mem_high(i):
                act.wait_ge(yh_f, i + 9)
                act.activation(yh[:, bass.ds(i + 4, 1), :], c_y[:].rearrange("p (a n) -> p a n", a=1), ACT.Copy
                               ).then_inc(yh_hi, 1)

            def mem_head(b, i, before):
                ahead(b, 0)
                unit_in(b, 1)
                act.wait_ge(att_s, i * 4 + 4 * A_MEM)
                act.activation(c_q[:], proj[0][:], ACT.Copy, scale=HEAD_SCALE).then_inc(bank_free[0], 1)
                if before:
                    mem_high(i - 1)
                exps(i + A_MEM, c_st, c_l, FULL, False)
                ahead(b, 2)
                unit_in(b, 3)
                act.wait_ge(yh_f, i + 8)
                act.activation(c_z[:], proj[1][:], ACT.Tanh, scale=0.5).then_inc(mem_act.sem, 1)
                copies(i + A_MEM, c_pt, FULL)

            mem_head(H4["mem"], 0, False)
            with act.Fori(1, MEM_HEADS) as i:
                mem_head(i + H4["mem"], i, True)
            mem_high(MEM_HEADS - 1)
            phase_end()

            with act.Fori(0, 4) as i:
                b, qb = i * 5 + H4["merge_sm"], i * 8 + Q2["merge_sm"]
                for t in range(4):
                    ahead(b, 5 * t, 5, (2, i * 64 + 16 * t + 16))
                    for x, branch in enumerate((1, 3)):
                        unit_in(b, 5 * t + 1 + 2 * x)
                        need(act, bank_free[x], qb + 2 * t)
                        act.activation(e_th[x][:], proj[x][:], ACT.Tanh, scale=0.5,
                                       bias=par[:, bass.ds(i * 4 + PARAM["b_merge"] + branch * KT + t, 1)]
                                       ).then_inc(bank_free[x], 1)
            phase_end()
            act.dma_start(p_w[:].rearrange("p g c d n -> p (g c) (d n)"),
                          a["w_pool_2"][0].rearrange("g (c p) n -> p (g c) n", p=P)).then_inc(weights_in, 16)

            for g in range(POOL_GROUPS):
                for u in range(4):
                    ahead(H4["pool"], 8 * g + 2 * u)
                    unit_in(H4["pool"], 8 * g + 2 * u + 1)
                    if u < 2:
                        if g:
                            wait(act, pool_dve, "p", g - 1)
                        act.activation(p_u[u][:, 16:16 + T], proj[u][:], ACT.Copy).then_inc(bank_free[u], 1)
                    else:
                        x = u - 2
                        if g or x:
                            act.wait_ge(yh_ready, YH_POOL + 2 * g + x)
                        act.activation(p_z[:], proj[x][:], ACT.Tanh, scale=0.5).then_inc(pool_act.sem, 1)
                        wait(act, pool_dve, f"y{x}", g)
                        act.activation(yh[:, 2 * g + x, :], p_z[:], ACT.Copy, scale=0.5).then_inc(pool_act.sem, 1)
            phase_end()
            merge("merge_p", 0)

            act.wait_ge(half_done, 4 * H4["wout2"])
            act.wait_ge(merged_done, 1)
            for k in range(KT):
                act.activation(ht_hi[:, k, :], xy[:, k, :], ACT.Copy, scale=0.5).then_inc(norm_hi, 1)
            phase_end()

            act.dma_start(x3[:], x2_spill.rearrange("k p t -> p k t")).then_inc(x2_in, 16)
            act.dma_start(f_rs[:], root_spill).then_inc(x2_in, 16)

            def wout2_iter(b, i):
                for u in range(2):
                    ahead(b, 2 * u)
                    unit_in(b, 2 * u + 1)
                    n = i * 2 + u
                    act.activation(xy[:, bass.ds(n, 1), :], proj[u][:].rearrange("p (a n) -> p a n", a=1),
                                   ACT.Copy).then_inc(y2_tile, 1)
                    squares(proj[u][:], f_sq[:], n + Z_Y2)
                    act.wait_ge(norm_sq, Z_Y2 + n + 1)
                    act.wait_ge(y2_tile, n + 1)
                    act.sem_inc(bank_free[u], 1)

            with act.Fori(0, KT // 2 - 1) as i:
                wout2_iter(i + H4["wout2"], i)
            wout2_iter(KT // 2 - 1 + H4["wout2"], KT // 2 - 1)
            nt = {"rstd": f_rstd}
            root(5)
            for k in range(KT):
                act.wait_ge(fin_pe, k + 1)
                act.activation(y_tok[:, :, k * P:(k + 1) * P], S[k % 4][:].rearrange("p (t n) -> p t n", n=P),
                               ACT.Copy).then_inc(fin_copy, 1)

        @block.vector
        def _(dve):
            link = Chain(dve, dve_chain)
            MUL, ADD, SUB, MAX, MIN = ALU.mult, ALU.add, ALU.subtract, ALU.max, ALU.min

            def unit_in(b, j):
                dve.wait_ge(half_done, th(b, j))

            def taken(qb, q):
                dve.wait_ge(bank_free[q % 2], qb + q // 2 + 1)

            phase = [0]

            def phase_end():
                phase[0] += 1
                dve.wait_ge(dve_chain, link.base + link.n)
                dve.sem_inc(dve_phase, 1)
                dve.wait_ge(act_phase, phase[0])

            def four(ap):
                return ap.rearrange("p (c n) -> p c n", n=P)

            dve.wait_ge(consts_built, CONSTS)
            wait(dve, pro_pe, "params")
            dve.tensor_copy(par[:], TB[0][:, 0:NPARAM]).then_inc(pro_dve.sem, 1)
            wait(dve, pro_dve, "params")
            wait(dve, pro_act, "root")
            dve.reciprocal(mem_rstd, mem_rstd).then_inc(pro_dve.sem, 1)
            wait(dve, pro_dve, "rstd")
            for t in (0, 1):
                dve.tensor_scalar(mem_tok[:, t, :], mem_tok[:, t, :], mem_rstd[:, t:t + 1], None, MUL
                                  ).then_inc(mem_scaled, 1)
            bm = par[:, PARAM["b_merge"]:PARAM["b_merge"] + 64]
            link(dve.tensor_scalar(bm, bm, 0.5, None, MUL))
            gp, gf = [par[:, PARAM[n]:PARAM[n] + KT] for n in ("g_pre", "final_norm_g")]
            link(dve.tensor_tensor(gp, gp, gf, MUL))
            p0 = PARAM["lru_ba"]
            link(dve.tensor_scalar(lru_hba, par[:, p0:p0 + 4], 0.5, None, MUL))
            p0 = PARAM["lru_bx"]
            link(dve.tensor_scalar(lru_hbx, par[:, p0:p0 + 4], 0.5, None, MUL))
            for k in range(KT):
                dve.wait_ge(memt_hi, k + 1)
                dve.wait_ge(act_chain, 4 + k + 1)
                link.inc(dve.scalar_tensor_tensor(ht_lo[:, k, 0:M], S[k % 4][:, 0:M], col("mem_norm_g", k),
                                                  ht_hi[:, k, 0:M].bitcast(F32), MUL, SUB))
                dve.scalar_tensor_tensor(ht_lo[:, k, M:T], S[k % 4][:, M:T], col("g_mem", k),
                                         ht_hi[:, k, M:T].bitcast(F32), MUL, SUB).then_inc(ht_ready, 1)

            def add_square(n, sq, acc, first):
                dve.wait_ge(norm_sq, n + 1)
                if first:
                    dve.tensor_copy(acc[:], sq[:]).then_inc(norm_acc, 1)
                else:
                    dve.wait_ge(norm_acc, n)
                    dve.tensor_tensor(acc[:], acc[:], sq[:], ADD).then_inc(norm_acc, 1)

            for k in range(KT):
                dve.wait_ge(xt_pe, k + 1)
                if k == 0:
                    dve.wait_ge(memt_pe, KT)
                dve.tensor_copy(x_t[:, k, :], S[k % 4][:]).then_inc(xt_x, 1)
                if k:
                    add_square(Z_X + k - 1, p_sq, p_acc, k == 1)
            add_square(Z_X + KT - 1, p_sq, p_acc, False)

            def kv(b, qb, i, vs):
                unit_in(b, 3)
                dve.tensor_copy(kv_v[:], proj[1][:, 0:M]).then_inc(bank_free[1], 1)
                dve.wait_ge(kv_t, qb + 1)
                dve.tensor_copy((v1, v2)[vs][:, i, :, :], TB[0][:, 0:M].rearrange("p (c n) -> p c n", n=P)
                                ).then_inc(v1_done, 1)

            def inverse(n, rstd):
                dve.wait_ge(norm_root, n)
                link(dve.reciprocal(rstd[:], rstd[:]))

            kv(0, 0, 0, 0)
            inverse(1, n0[0])
            with dve.Fori(1, 4) as i:
                kv(i, i, i, 0)
            with dve.Fori(0, 4) as i:
                kv(i + 4, i + 4, i, 1)

            def normed(x, gain, rstd, t, base, ht0):
                for k in range(KT):
                    if k >= 2:
                        dve.wait_ge(ht_ready, ht0 + k - 1)
                    dve.scalar_tensor_tensor(t[k % 2][:], x[:, k, :], col(gain, k), rstd[:], MUL, MUL).then_inc(norm_t, 1)
                    if k:
                        low(t, base, ht0, k - 1)
                low(t, base, ht0, KT - 1)

            def low(t, base, ht0, k):
                dve.wait_ge(norm_hi, ht0 - KT + k + 1)
                dve.wait_ge(norm_t, base + k + 1)
                dve.tensor_tensor(ht_lo[:, k, :], t[k % 2][:], ht_hi[:, k, :].bitcast(F32), SUB).then_inc(ht_ready, 1)

            normed(x_t, "mix_norm_g", n0[0], n0[1:3], 0, HT_X)
            phase_end()
            dve.wait_ge(lru_lam, 1)
            lam = par[:, PARAM["lru_lambda"]:PARAM["lru_lambda"] + 4]
            link(dve.tensor_scalar(lam, lam, -1.0, 0.0, MUL, MAX))
            link(dve.tensor_tensor(lam, lam, lru_half_c, ADD))
            dve.tensor_scalar(lru_half_c, lam, -2.0, None, MUL).then_inc(lru_c, 1)
            link(dve.memset(l_xp[:, 0:3], 0.0))

            def conv(dst, src, w0, bias):
                link(dve.tensor_scalar(dst, src[:, 0:T], w0(0), bias, MUL, ADD))
                for j in range(1, 4):
                    ins = dve.scalar_tensor_tensor(dst, src[:, j:j + T], w0(j), dst, MUL, ADD)
                    if j < 3:
                        link(ins)
                return ins

            def lru_iter(b, qb, i):
                link(dve.tensor_copy(l_w[:, 0, :], lru_wa[:, bass.ds(i, 1), :].rearrange("p a n -> p (a n)")))
                link(dve.tensor_copy(l_w[:, 1, :], lru_wx[:, bass.ds(i, 1), :].rearrange("p a n -> p (a n)")))
                taken(qb, 0)

                def tap(j):
                    return par[:, bass.ds(i + PARAM["lru_conv_w"] + 4 * j, 1)]
                conv(l_xc[:], l_xp, tap, par[:, bass.ds(i + PARAM["lru_conv_b"], 1)]).then_inc(lru_dve.sem, 1)
                wait(dve, lru_act, "t", i)
                link(dve.tensor_scalar(l_rd[:], l_t[:], -1.0, 1.0, MUL, ADD))
                link(dve.reciprocal(l_rd[:], l_rd[:]))
                link(dve.scalar_tensor_tensor(l_q[:], l_t[:], -2.0, l_rd[:], MUL, MUL))
                link.inc(dve.tensor_scalar(l_a[:], l_q[:], -1.0, 1.0, MUL, ADD))
                dve.scalar_tensor_tensor(l_s[:], l_q[:], 2.0, l_q[:], SUB, MUL).then_inc(lru_dve.sem, 1)
                wait(dve, lru_dve, "xc", i)
                link(dve.scalar_tensor_tensor(l_ti[:], l_ti[:], 1.0, l_xc[:], ADD, MUL))
                wait(dve, lru_act, "z", i)
                dve.scalar_tensor_tensor(l_sz[:], l_tz[:], 1.0, proj[1][:], ADD, MUL).then_inc(bank_free[1], 1)
                wait(dve, lru_act, "root", i)
                link(dve.scalar_tensor_tensor(l_h[:], l_ti[:], 0.5, l_h[:], MUL, MUL))
                link(dve.tensor_tensor_scan(l_tr[:], l_a[:], l_h[:], 0.0, MUL, ADD))
                taken(qb, 1)
                dve.scalar_tensor_tensor(xy[:, i, :], l_sz[:], 0.5, l_tr[:], MUL, MUL).then_inc(lru_dve.sem, 1)

            lru_iter(H4["lru"], Q2["lru"], 0)
            with dve.Fori(1, LRU_BLOCKS) as i:
                link.enter(i - 1, 12)
                wait(dve, lru_dve, "y", i - 1)
                lru_iter(i + H4["lru"], i + Q2["lru"], i)
            link.leave(3)
            wait(dve, lru_dve, "y", LRU_BLOCKS - 1)
            phase_end()

            link.inc(dve.memset(m_g[:], 0.0))
            link.inc(dve.memset(m_q[64:P, 1, :], 0.0))
            link.inc(dve.memset(m_q[0:64, 2, :], 0.0))
            link.inc(dve.memset(m_up[:, 0:3], 0.0))
            link.inc(dve.memset(m_v[:, :, :, ML_DH:ML_DH + 1], 1.0))
            link.inc(dve.tensor_scalar(m_neg[:], dist[:, T - P:T], 0.0, -1e30, ALU.is_lt, MUL))
            block_of = dist[:, T - P:T].rearrange("p (b o) -> p b o", o=4)[:, :, 0:1].to_broadcast([P, 32, 4])
            mask4 = m_bdmask[:].rearrange("p (b o) -> p b o", o=4)
            link(dve.tensor_scalar(mask4, block_of, 0.0, None, ALU.is_le))
            link(dve.scalar_tensor_tensor(mask4, block_of, -3.0, mask4, ALU.is_ge, MUL))
            dve.wait_ge(half_done, 4 * H4["mlg"] + 4)
            dve.tensor_copy(gate_rows[0:8, :], S[3][0:8, :]).then_inc(ml_gate.sem, 1)
            hb, qb = H4["ml"], Q2["ml"]
            for pr in range(ML_PAIRS):
                order = [0]

                def signal(ins, name):
                    assert ml_dve.names.index(name) == order[0], name
                    order[0] += 1
                    ins.then_inc(ml_dve.sem, 1)

                h0, q0 = 18 * pr, 9 * pr
                dve.wait_ge(weights_in, 16 * 5)
                if pr:
                    wait(dve, ml_pe, "y2", pr - 1)
                for m in range(3):
                    for x in range(3):
                        src = m_wd[:, m, 3 * pr + x:3 * pr + x + 1, :].to_broadcast([P, 32, 4])
                        link.inc(dve.tensor_tensor(m_bd[:, m, x, :].rearrange("p (b o) -> p b o", o=4), src, mask4, MUL))
                dve.wait_ge(dve_chain, link.base + link.n)

                def ml_conv_silu(x):
                    q = q0 + x
                    taken(qb, q)
                    if x:
                        wait(dve, ml_pe, f"qk{x - 1}", pr)
                    k = 3 * pr + x
                    conv(m_uc[:], m_up, lambda j: par[:, PARAM["ml_conv_w"] + 6 * j + k:PARAM["ml_conv_w"] + 6 * j + k + 1],
                         col("ml_conv_b", k)).then_inc(ml_conv, 1)
                    wait(dve, ml_act, f"th{x}", pr)
                    signal(dve.scalar_tensor_tensor(m_uc[:], m_hf[:, x * T:(x + 1) * T], 1.0, m_uc[:], ADD, MUL), f"uc{x}")

                def ml_kv(x):
                    wait(dve, ml_pe, f"qk{x}", pr)
                    signal(dve.tensor_scalar(m_k[:, x, :], S[1][:], 0.5 * ML_DH ** -0.5, None, MUL), f"k{x}")
                    signal(dve.tensor_copy(m_hf[:, x * T:(x + 1) * T], S[2][:]), f"v{x}")

                def ml_ot(x):
                    wait(dve, ml_pe, f"o{x}", pr)
                    t0 = four(TB[0][:])
                    if x == 0:
                        ins = dve.tensor_scalar(m_h[:, :, 0, 0:P], t0, 1.0, None, ADD)
                    elif x == 1:
                        link.inc(dve.tensor_scalar(m_h[:, :, 0, P:ML_DH], t0[:, :, 0:64], 1.0, None, ADD))
                        ins = dve.tensor_scalar(m_h[:, :, 1, 0:64], t0[:, :, 64:P], 1.0, None, ADD)
                    else:
                        ins = dve.tensor_scalar(m_h[:, :, 1, 64:ML_DH], t0, 1.0, None, ADD)
                    signal(ins, f"ot{x}")

                def ml_weights(c):
                    wait(dve, ml_act, f"e{c}", pr)
                    signal(dve.tensor_tensor(m_e[:], S[0][:, 0:2 * P].rearrange("p (h n) -> p h n", n=P), m_e[:], MUL),
                           f"se{c}")

                def ml_core(c):
                    n = ML_DH + 1
                    wait(dve, ml_act, f"tot{c}", pr)
                    if c:
                        s2 = S[2][:].rearrange("p (h n) -> p h n", n=256)[:, :, 0:n]
                        link(dve.tensor_tensor(m_tot[:], m_tot[:], s2, ADD))
                    if c < NT - 1:
                        wait(dve, ml_pe, f"cu{c}", pr)
                        parts = [(m_c[:, 0, :], TB[1][:, 0:n], 0, slice(0, P)),
                                 (m_c[0:64, 1, :], TB[1][0:64, 256:256 + n], 0, slice(0, 64)),
                                 (m_c[64:P, 1, :], TB[1][64:P, 256:256 + n], 1, slice(64, P)),
                                 (m_c[:, 2, :], TB[0][:, 0:n], 1, slice(0, P))]
                        for k, (dst, src, hh, rows) in enumerate(parts):
                            if c == 0:
                                ins = dve.tensor_copy(dst, src)
                            else:
                                ins = dve.scalar_tensor_tensor(dst, dst, m_sm[rows, 16 + 4 * hh + c:17 + 4 * hh + c],
                                                               src, MUL, ADD)
                            if k < 3:
                                link.inc(ins)
                        signal(ins, f"c{c}")
                    den, dd = m_tot[:, :, ML_DH], m_sm[:, 48:50]
                    link(dve.scalar_tensor_tensor(dd, den, -1.0, m_gc[:, c, 64:66], MUL, MAX))
                    link(dve.tensor_tensor(dd, dd, den, MAX))
                    link(dve.reciprocal(dd, dd))
                    link(dve.tensor_tensor(m_h[:, c, :, :], m_h[:, c, :, :], m_tot[:, :, 0:ML_DH], MUL))
                    for hh in range(2):
                        h = m_h[:, c, hh, :]
                        link(dve.tensor_scalar(h, h, dd[:, hh:hh + 1], 0.5, MUL, MUL))
                        link(dve.bn_stats(m_sm[:, 50:56], h))
                        link(dve.bn_aggr(m_mv[:, 2 * c + hh, :], m_sm[:, 50:56]))

                def ml_z(x):
                    wait(dve, ml_act, f"z{x}", pr)
                    q = q0 + 6 + x
                    t = xy[:, 4 + 3 * pr + x, :]
                    dve.scalar_tensor_tensor(t, t, 1.0, proj[q % 2][:], ADD, MUL).then_inc(bank_free[q % 2], 1)

                ml_conv_silu(0)
                wait(dve, ml_act, "ln", pr)
                link(dve.scalar_tensor_tensor(r_f[0:2, :], r_f[0:2, :], 0.0, r_b[0:2, :], MIN, SUB))
                for c in range(NT):
                    cc = slice(c * P, (c + 1) * P)
                    link(dve.tensor_tensor_scan(r_b[0:2, cc], ones[0:2, :], r_f[0:2, cc], 0.0, MUL, ADD))
                link(dve.tensor_tensor(m_g[0:2, :], r_ig[0:2, :], r_b[0:2, :], SUB))
                link(dve.memset(m_sm[0:2, 0:1], 0.0))
                for c in range(NT):
                    cc = slice(c * P, (c + 1) * P)
                    e = c * P + P - 1
                    link(dve.tensor_tensor_scan(r_r[0:2, cc], m_g[0:2, cc], m_g[0:2, cc], m_sm[0:2, c:c + 1], MAX, MAX))
                    link(dve.tensor_tensor(m_sm[0:2, c + 1:c + 2], r_b[0:2, e:e + 1], r_r[0:2, e:e + 1], ADD))
                link(dve.tensor_scalar(r_r[0:2, :], r_r[0:2, :], -1.0, None, MUL))
                last = r_r[0:2, :].rearrange("p (c n) -> p c n", n=P)[:, :, P - 1]
                link(dve.tensor_tensor(m_sm[0:2, 8:12], m_sm[0:2, 0:4], last, ADD))
                signal(dve.tensor_tensor(r_ig[0:2, :], r_r[0:2, :], r_b[0:2, :], SUB), "rows")
                ml_kv(0)
                ml_conv_silu(1)
                ml_kv(1)
                ml_conv_silu(2)
                wait(dve, ml_pe, "sold", pr)
                signal(dve.tensor_copy(m_sm[:, 16:24], S[3][:, 0:8]), "sold")
                ml_kv(2)
                wait(dve, ml_pe, "v2", pr)
                ml_ot(0)
                ml_ot(1)
                ml_ot(2)
                ml_weights(0)
                ml_z(0)
                ml_core(0)
                ml_weights(1)
                ml_z(1)
                ml_z(2)
                ml_core(1)
                for c in (2, 3):
                    ml_weights(c)
                    ml_core(c)
                dve.sem_inc(ml_var, 1)
                wait(dve, ml_act, "root", pr)
                rs = m_sm[:, 24:32]
                link(dve.reciprocal(rs, rs))
                link(dve.tensor_scalar(rs, rs, 0.5, None, MUL))
                for k in range(8):
                    h = m_h[:, k // 2, k % 2, :]
                    ins = dve.tensor_scalar(h, h, m_mv[:, k, 0:1], rs[:, k:k + 1], SUB, MUL)
                    if k < 7:
                        link.inc(ins)
                signal(ins, "hn")
                for x in range(3):
                    wait(dve, ml_pe, f"y{x}", pr)
                    t = xy[:, 4 + 3 * pr + x, :]
                    q = q0 + 6 + x
                    taken(qb, q)
                    ins = dve.scalar_tensor_tensor(t, S[x][:], col("ml_norm_g", 3 * pr + x), t, MUL, MUL)
                    if x < 2:
                        link.inc(ins)
                signal(ins, "y")
            wait(dve, ml_dve, "y", ML_PAIRS - 1)
            phase_end()

            def logits(n, st, l, geo, strip=None, slope=None, s0=0):
                offs = [sum(g[1] for g in geo[:t]) * P for t in range(NT)]
                for t, (b0, nb) in enumerate(geo):
                    dve.wait_ge(att_s, n * 4 + t + 1)
                    src = S[t][:, 0:nb * P]
                    if strip is not None:
                        lt = l[:, offs[t]:offs[t] + nb * P]
                        c0 = (T - P) - P * (t - b0) - s0
                        link(dve.scalar_tensor_tensor(lt, strip[:, c0:c0 + nb * P], slope, src, MUL, ADD))
                        src = lt
                    dve.tensor_reduce(st[:, t:t + 1], src, AX, MAX, negate=True).then_inc(att_l, 1)

            def keys(k, bank, free):
                for t in range(NT):
                    tt = slice(t * P, (t + 1) * P)
                    dve.tensor_copy(k[:, tt], bank[:, tt]).then_inc(att_k if t < NT - 1 else free, 1)

            def out_tokens(n, st, o):
                dve.wait_ge(att_o, n + 1)
                link(dve.reciprocal(st[:, 8:12], st[:, 4:8]))
                for t in range(NT):
                    ins = dve.tensor_scalar(o[:, t * P:(t + 1) * P], S[0][:, t * P:(t + 1) * P], st[:, 8 + t:9 + t], None, MUL)
                    if t < NT - 1:
                        link.inc(ins)
                ins.then_inc(att_ok, 1)

            link(dve.tensor_scalar(a_strip[:], dist[:], 0.0, MASKED, ALU.is_gt, MUL))
            link(dve.tensor_tensor(a_strip[:], a_strip[:], dist[:], ADD))
            dve.sem_inc(att_ok, 1)
            dve.sem_inc(att_y, 1)
            with dve.Fori(0, MO_HEADS) as i:
                link.enter(i, 9)
                b, qb = i * 2 + H4["moba"], i * 2 + Q2["moba"]
                unit_in(b, 5)
                keys(a_k, proj[0], bank_free[0])
                logits(i, a_st, a_l, CAUSAL, a_strip, mo_slopes[:, bass.ds(i, 1)])
                wait(dve, moz_act, "z", i)
                link(dve.scalar_tensor_tensor(a_z[:], a_z[:], 1.0, proj[1][:], ADD, MUL))
                dve.sem_inc(bank_free[1], 1)
                out_tokens(i, a_st, a_o)
                dve.wait_ge(att_ot, i + 1)
                dve.scalar_tensor_tensor(xy[:, i + 10, :], a_z[:], 0.5, TB[0][:], MUL, MUL).then_inc(att_y, 1)
            link.leave(MO_HEADS)

            def lows(x, ht0, scale):
                for k in range(KT):
                    dve.wait_ge(norm_hi, ht0 - KT + k + 1)
                    hi = ht_hi[:, k, :].bitcast(F32)
                    if scale is None:
                        ins = dve.tensor_tensor(ht_lo[:, k, :], x[:, k, :], hi, SUB)
                    else:
                        ins = dve.scalar_tensor_tensor(ht_lo[:, k, :], x[:, k, :], scale, hi, MUL, SUB)
                    ins.then_inc(ht_ready, 1)

            dve.wait_ge(att_y, MO_HEADS + 1)
            lows(xy, HT_Y, None)
            dve.wait_ge(ht_ready, HT_Y + KT)
            phase_end()

            link(dve.memset(n_acc[:], 0.0))
            with dve.Fori(0, KT // 2) as i:
                for u in range(2):
                    n = i * 2 + u
                    b = i + H4["wout"]
                    unit_in(b, 2 * u + 1)
                    dve.wait_ge(tile_in[u], i * 16 + 16)
                    dve.tensor_tensor(xy[:, n, :], proj[u][:], n_x[u][:], ADD).then_inc(bank_free[u], 1)
                    dve.wait_ge(norm_sq, n + Z_X1 + 1)
                    dve.wait_ge(norm_acc, n + Z_X1)
                    dve.tensor_tensor(n_acc[:], n_acc[:], n_sq[:], ADD).then_inc(norm_acc, 1)
            inverse(2, n_rstd)
            normed(xy, "xa_norm_g", n_rstd, [n_t0, n_t1], KT, HT_X1)

            def rounded(y, hi, lo, y_from):
                dve.wait_ge(yh_hi, y_from)
                dve.tensor_tensor(lo, y, hi.bitcast(F32), SUB).then_inc(yh_ready, 1)

            dve.wait_ge(ht_ready, HT_X1 + KT)
            for h in range(XA_HEADS + 1):
                if h:
                    out_tokens(A_XA + h - 1, b_st, b_o)
                    dve.wait_ge(att_ot, A_XA + h)
                    dve.tensor_copy(n_t0[:], TB[0][:]).then_inc(yh_f, 1)
                    rounded(n_t0[:], o_hi[:, h - 1, :], o_lo[:, h - 1, :], h)
                if h < XA_HEADS:
                    logits(A_XA + h, b_st, b_l, FULL)
            link(dve.memset(n_acc[:], 0.0))
            link(dve.memset(n_acc3[:], 0.0))
            with dve.Fori(0, 2) as i:
                for q in range(8):
                    n = i * 8 + q
                    m = i * 16 + 2 * q + Z_X2
                    if q % 2:
                        unit_in(i + H4["xwo"], q // 2)
                    else:
                        dve.wait_ge(part_done, i * 4 + q // 2 + 1)
                    dve.tensor_tensor(xy[:, n, :], proj[q % 2][:], xy[:, n, :], ADD).then_inc(bank_free[q % 2], 1)
                    dve.wait_ge(norm_sq, m + 1)
                    dve.wait_ge(norm_acc, m)
                    dve.tensor_tensor(n_acc[:], n_acc[:], n_sq[:], ADD).then_inc(norm_acc, 1)
                    dve.wait_ge(norm_sq, m + 2)
                    dve.tensor_tensor(n_acc3[:], n_acc3[:], n_sq3[:], ADD).then_inc(norm_acc, 1)
            dve.sem_inc(x2_done, 1)
            dve.wait_ge(norm_sum, 4)
            link(dve.tensor_scalar(n_rs[:], TB[1][:], 1.0 / D, RMS_EPS, MUL, ADD))
            dve.scalar_tensor_tensor(n_rstd[:], n_rs[:], RMS_EPS * D, TB[0][:], MUL, ADD).then_inc(norm_v, 1)
            inverse(3, n_rstd)
            normed(xy, "g_pre", n_rstd, [n_t0, n_t1], 2 * KT, HT_H2)
            dve.wait_ge(ht_ready, HT_H2 + KT)
            phase_end()
            phase_end()

            gm = g_mask[:, 0, :]
            link(dve.tensor_scalar(gm, dist[:, T - P:T], 0.0, None, ALU.is_ge))
            link(dve.memset(g_mask[0:64, 0, 64:P], 0.0))
            for c in range(1, 4):
                link(dve.tensor_copy(g_mask[:, c, :], gm))
            link(dve.memset(g_at[:], 0.0))
            dve.wait_ge(half_done, 4 * H4["glr"] + 4)
            link(dve.tensor_copy(g_lr[:], S[3][0:16, :]))
            dve.wait_ge(weights_in, 16 * 6)
            dve.tensor_copy(g_wh[:], g_wal[:, 0:P]).then_inc(gla_wh, 1)

            def gla_head(b, i, more):
                wait(dve, gla_act, "ln", i)
                if more:
                    dve.tensor_copy(g_wh[:], g_wal[:, bass.ds((i + 1) * P, P)]).then_inc(gla_wh, 1)
                link(dve.scalar_tensor_tensor(g_x[:], g_x[:], 0.0, g_e[:], MIN, SUB))
                for c in range(8):
                    cc = slice(c * 64, (c + 1) * 64)
                    link(dve.tensor_tensor_scan(g_b[:, cc], ones[:, 0:64], g_x[:, cc], 0.0, MUL, ADD))
                b8 = g_b[:].rearrange("p (c n) -> p c n", n=64)
                dve.tensor_tensor(g_x[:].rearrange("p (c n) -> p c n", n=64), b8[:, :, 63:64].to_broadcast([P, 8, 64]),
                                  b8, SUB).then_inc(gla_dve.sem, 1)
                wait(dve, gla_act, "ex", i)
                unit_in(b, 1)
                dve.scalar_tensor_tensor(g_qt[:], proj[0][:], GLA_DK ** -0.5, g_e[:], MUL, MUL).then_inc(bank_free[0], 1)
                unit_in(b, 3)
                dve.tensor_tensor(g_kt[:], proj[1][:], g_y[:], MUL).then_inc(gla_dve.sem, 1)
                link(dve.tensor_tensor(g_kk[:], proj[1][:], g_x[:], MUL))
                dve.wait_ge(gla_dve.sem, gla_dve.value("kt", i))
                dve.sem_inc(bank_free[1], 1)
                dve.sem_inc(gla_dve.sem, 1)
                wait(dve, gla_pe, "va", i)
                dve.tensor_copy(g_vt[:, :, 0:P], four(TB[1][:])).then_inc(gla_dve.sem, 1)
                wait(dve, gla_pe, "vb", i)
                wait(dve, gla_pe, "at", i)
                dve.tensor_copy(g_vt[:, :, P:2 * P], four(TB[0][:])).then_inc(gla_dve.sem, 1)
                dve.copy_predicated(g_at[:], g_mask[:].bitcast(U32), four(S[0][:])).then_inc(gla_dve.sem, 1)
                for x in range(2):
                    wait(dve, gla_act, f"z{x}", i)
                    link(dve.scalar_tensor_tensor(g_z[:, x, :], g_z[:, x, :], 1.0, proj[x][:], ADD, MUL))
                    dve.sem_inc(bank_free[x], 1)
                    if x == 0:
                        wait(dve, gla_pe, "kv", i)
                        for c in range(7):
                            src = gla_kv(c)
                            if c == 0:
                                link(dve.tensor_copy(g_st[:, 0, :], src))
                            else:
                                ins = dve.scalar_tensor_tensor(g_st[:, c, :], g_st[:, c - 1, :], g_dec[:, c:c + 1], src, MUL, ADD)
                                if c < 6:
                                    link(ins)
                        ins.then_inc(gla_dve.sem, 1)
                wait(dve, gla_act, "root", i)
                link(dve.reciprocal(g_ss[:, 4:8], g_ss[:, 4:8]))
                link(dve.tensor_scalar(g_ss[:, 4:8], g_ss[:, 4:8], 0.5, None, MUL))
                for p2 in range(4):
                    o = (S[0], TB[0])[p2 // 2][:, (p2 % 2) * 256:(p2 % 2) * 256 + 256]
                    ins = dve.tensor_scalar(g_o[:, p2, :], o, g_ss[:, 4 + p2:5 + p2], None, MUL)
                    if p2 < 3:
                        link.inc(ins)
                ins.then_inc(gla_dve.sem, 1)
                wait(dve, gla_pe, "ot", i)
                for x in range(2):
                    dve.scalar_tensor_tensor(g_y[:], S[1 + x][:], par[:, bass.ds(i * 2 + PARAM["g_gla"] + x, 1)],
                                             g_z[:, x, :], MUL, MUL).then_inc(gla_dve.sem, 1)
                    wait(dve, gla_act, f"hi{x}", i)
                    wait(dve, gla_dve, f"y{x}", i)
                    ins = dve.tensor_tensor(yl[:, i * 2 + x, :], g_y[:], yh[:, i * 2 + x, :].bitcast(F32), SUB)
                    ins.then_inc(yh_ready, 1)
                    dve.wait_ge(yh_ready, i * 2 + YH_GLA + x + 1)

            with dve.Fori(0, GLA_HEADS - 1) as i:
                link.enter(i, 23)
                gla_head(i * 3 + H4["gla"], i, True)
            link.leave(GLA_HEADS - 1)
            gla_head((GLA_HEADS - 1) * 3 + H4["gla"], GLA_HEADS - 1, False)
            phase_end()

            def merge(name, first):
                with dve.Fori(0, 4) as i:
                    link.enter(i, 0 if first else 4)
                    b, qb = i * 3 + H4[name], i * 4 + Q2[name]
                    for t in range(4):
                        n = i * 4 + t
                        unit_in(b, 3 * t + 2)
                        taken(qb, 2 * t)
                        dst = xy[:, n, :] if first else e_tmp[:]
                        dve.scalar_tensor_tensor(dst, e_th[t % 2][:], 1.0, proj[1][:], ADD, MUL).then_inc(bank_free[1], 1)
                        if not first:
                            dve.wait_ge(bank_free[1], qb + t + 1)
                            link(dve.tensor_tensor(xy[:, n, :], xy[:, n, :], e_tmp[:], ADD))
                link.leave(4)

            merge("merge_g", True)
            dve.wait_ge(bank_free[1], Q2["merge_g"] + 16)
            phase_end()

            link(dve.tensor_scalar(w_strip1[:], dist[:, 256:512], 0.0, MASKED, ALU.is_gt, MUL))
            link(dve.tensor_tensor(w_strip1[:], w_strip1[:], dist[:, 256:512], ADD))
            link(dve.tensor_scalar(w_l[:, 0:256], dist[:, 256:512], -128.0, MASKED, ALU.is_lt, MUL))
            link(dve.tensor_tensor(w_strip1[:], w_strip1[:], w_l[:, 0:256], ADD))
            ROUND = 1.5 * 2.0 ** 23
            for d, strip in ((4, w_strip4), (16, w_strip16)):
                t = w_l[:, 0:T]
                link(dve.tensor_scalar(t, dist[:], 1.0 / d, ROUND, MUL, ADD))
                link(dve.tensor_scalar(t, t, ROUND, float(d), SUB, MUL))
                link(dve.tensor_tensor(t, t, dist[:], ALU.not_equal))
                link(dve.scalar_tensor_tensor(strip[:], t, MASKED, dist[:], MUL, ADD))
                link(dve.tensor_scalar(t, dist[:], 0.0, MASKED, ALU.is_gt, MUL))
                link(dve.tensor_tensor(strip[:], strip[:], t, ADD))
            geo = (WINDOW, CAUSAL, CAUSAL)
            with dve.Fori(0, SWA_HPG) as i:
                link.enter(i, 38)
                b, qb = i * 5 + H4["swa"], i * 5 + Q2["swa"]
                for g in range(SWA_GROUPS + 1):
                    n = i * 3 + A_SWA + g
                    if g:
                        dve.wait_ge(att_o, n)
                        dve.tensor_copy(w_og[:, g - 1, :], S[0][:]).then_inc(att_ok, 1)
                    if g == SWA_GROUPS:
                        break
                    q = 3 * g + 2
                    unit_in(b, 6 * g + 5)
                    keys(w_k, proj[q % 2], bank_free[q % 2])
                    logits(n, w_st[:, 12 * g:12 * g + 12], w_l, geo[g], (w_strip1, w_strip4, w_strip16)[g],
                           swa_slopes[:, bass.ds(i + 4 * g, 1)], 256 if g == 0 else 0)
                nm = [w_st[:, 12 * g:12 * g + 4] for g in range(3)]
                den = [w_st[:, 12 * g + 4:12 * g + 8] for g in range(3)]
                top = w_st[:, 8:12]
                link(dve.tensor_tensor(top, nm[0], nm[1], MIN))
                link(dve.tensor_tensor(top, top, nm[2], MIN))
                for g in range(3):
                    link(dve.tensor_tensor(w_wt[:, 4 * g:4 * g + 4], top, nm[g], SUB))
                dve.sem_inc(comb_in, 1)
                wait(dve, comb_act, "w", i)
                for g in range(3):
                    link(dve.tensor_tensor(den[g], den[g], w_wt[:, 4 * g:4 * g + 4], MUL))
                link(dve.tensor_tensor(top, den[0], den[1], ADD))
                link(dve.tensor_tensor(top, top, den[2], ADD))
                link(dve.reciprocal(top, top))
                for g in range(3):
                    link(dve.tensor_tensor(w_wt[:, 4 * g:4 * g + 4], w_wt[:, 4 * g:4 * g + 4], top, MUL))
                dve.wait_ge(att_ok, i * 3 + A_SWA + 4)
                for g in range(3):
                    for t in range(NT):
                        tt = slice(t * P, (t + 1) * P)
                        r = w_wt[:, 4 * g + t:4 * g + t + 1]
                        if g == 0:
                            ins = dve.tensor_scalar(w_og[:, 0, tt], w_og[:, 0, tt], r, None, MUL)
                        else:
                            ins = dve.scalar_tensor_tensor(w_og[:, 0, tt], w_og[:, g, tt], r, w_og[:, 0, tt], MUL, ADD)
                        if g < 2 or t < NT - 1:
                            link.inc(ins)
                    if g < 2:
                        dve.wait_ge(dve_chain, link.base + link.n)
                ins.then_inc(comb_dve.sem, 1)
                wait(dve, comb_act, "z", i)
                link(dve.scalar_tensor_tensor(w_v[:], w_v[:], 1.0, proj[1][:], ADD, MUL))
                dve.sem_inc(bank_free[1], 1)
                dve.wait_ge(att_ot, i + A_SWA + 1)
                dve.scalar_tensor_tensor(w_q[:], w_v[:], 0.5, TB[0][:], MUL, MUL).then_inc(yh_f, 1)
                dve.wait_ge(yh_f, i + 5)
                rounded(w_q[:], yh[:, i, :], yl[:, i, :], i + 5)
            link.leave(SWA_HPG)
            dve.wait_ge(yh_ready, YH_SWA + 4)
            phase_end()

            with dve.Fori(0, MEM_HEADS) as i:
                link.enter(i, 5)
                logits(i + A_MEM, c_st, c_l, FULL)
                wait(dve, mem_act, "z", i)
                link(dve.scalar_tensor_tensor(c_z[:], c_z[:], 1.0, proj[1][:], ADD, MUL))
                dve.sem_inc(bank_free[1], 1)
                out_tokens(i + A_MEM, c_st, c_o)
                dve.wait_ge(att_ot, i + A_SWA + 5)
                dve.scalar_tensor_tensor(c_y[:], c_z[:], 0.5, TB[0][:], MUL, MUL).then_inc(yh_f, 1)
                dve.wait_ge(yh_f, i + 9)
                rounded(c_y[:], yh[:, i + 4, :], yl[:, i + 4, :], i + 9)
                dve.wait_ge(yh_ready, i + YH_MEM + 1)
            link.leave(MEM_HEADS)
            phase_end()

            with dve.Fori(0, 4) as i:
                link.enter(i, 8)
                b, qb = i * 5 + H4["merge_sm"], i * 8 + Q2["merge_sm"]
                for t in range(4):
                    n = i * 4 + t
                    for x in range(2):
                        if x:
                            unit_in(b, 5 * t + 4)
                        else:
                            dve.wait_ge(part_done, i * 4 + KT // 2 + t + 1)
                        taken(qb, 4 * t + x)
                        dve.scalar_tensor_tensor(e_tmp[:], e_th[x][:], 1.0, proj[x][:], ADD, MUL).then_inc(bank_free[x], 1)
                        dve.wait_ge(bank_free[x], qb + 2 * t + 2)
                        link(dve.tensor_tensor(xy[:, n, :], xy[:, n, :], e_tmp[:], ADD))
            link.leave(4)
            phase_end()

            for tile in (*p_u, *p_s):
                link.inc(dve.memset(tile[:, 0:16], 0.0))
            for g in range(POOL_GROUPS):
                w = 2 << g
                link(dve.tensor_scalar(p_rc[:, g, :], count16[:], float(w), None, MIN))
                link(dve.reciprocal(p_rc[:, g, :], p_rc[:, g, :]))
            for g in range(POOL_GROUPS):
                w = 2 << g
                for x in range(2):
                    taken(Q2["pool"], 4 * g + x)
                    if g:
                        wait(dve, pool_pe, "mix", g - 1)
                    src, d = p_u[x], 1
                    while d < w:
                        dst = p_s[0] if src is not p_s[0] else p_s[1]
                        link(dve.tensor_tensor(dst[:, 16:16 + T], src[:, 16:16 + T], src[:, 16 - d:16 - d + T], ADD))
                        src, d = dst, 2 * d
                    u = p_u[x]
                    link(dve.scalar_tensor_tensor(p_p[x][:], src[:, 16:16 + T], 1.0 / w, u[:, 16:16 + T], MUL, SUB))
                    link(dve.tensor_tensor(p_p[x][:, 0:16], src[:, 16:32], p_rc[:, g, :], MUL))
                    ins = dve.tensor_tensor(p_p[x][:, 0:16], p_p[x][:, 0:16], u[:, 16:32], SUB)
                    if x == 0:
                        link(ins)
                ins.then_inc(pool_dve.sem, 1)
                for x in range(2):
                    wait(dve, pool_act, f"z{x}", g)
                    link(dve.scalar_tensor_tensor(p_z[:], p_z[:], 1.0, proj[x][:], ADD, MUL))
                    dve.sem_inc(bank_free[x], 1)
                    wait(dve, pool_pe, "mix", g)
                    dve.scalar_tensor_tensor(p_z[:], S[x][:], col("pool_scale", 2 * g + x), p_z[:], MUL, MUL
                                             ).then_inc(pool_dve.sem, 1)
                    wait(dve, pool_act, f"hi{x}", g)
                    wait(dve, pool_dve, f"y{x}", g)
                    dve.scalar_tensor_tensor(yl[:, 2 * g + x, :], p_z[:], 0.5, yh[:, 2 * g + x, :].bitcast(F32), MUL, SUB
                                             ).then_inc(yh_ready, 1)
            dve.wait_ge(yh_ready, YH_END)
            phase_end()
            merge("merge_p", False)
            dve.sem_inc(merged_done, 1)
            lows(xy, HT_MERGED, 0.5)
            dve.wait_ge(ht_ready, HT_MERGED + KT)
            phase_end()
            link(dve.memset(f_acc[:], 0.0))

            def y2_square(i):
                dve.wait_ge(norm_sq, i + Z_Y2 + 1)
                dve.wait_ge(norm_acc, i + Z_Y2)
                dve.tensor_tensor(f_acc[:], f_acc[:], f_sq[:], ADD).then_inc(norm_acc, 1)

            y2_square(0)
            dve.wait_ge(x2_in, 32)
            link(dve.reciprocal(f_rs[:], f_rs[:]))
            with dve.Fori(1, KT) as i:
                y2_square(i)
                link.enter(i - 1, 1)
                x = x3[:, i - 1, :]
                link.inc(dve.scalar_tensor_tensor(x, x, par[:, bass.ds(i - 1 + PARAM["final_norm_g"], 1)], f_rs[:], MUL, MUL))
            link.leave(KT - 1)
            x = x3[:, KT - 1, :]
            link(dve.scalar_tensor_tensor(x, x, col("final_norm_g", KT - 1), f_rs[:], MUL, MUL))
            inverse(5, f_rstd)
            for k in range(KT):
                t = xy[:, k, :]
                link(dve.scalar_tensor_tensor(t, t, col("g_post", k), f_rstd[:], MUL, MUL))
                dve.tensor_tensor(t, t, x3[:, k, :], ADD).then_inc(fin_dve, 1)


_INS = ["x", "mem", "mix_norm_g", "w_in", "lru_conv_w", "lru_conv_b", "lru_wa", "lru_ba", "lru_wx", "lru_bx",
        "lru_lambda", "ml_conv_w", "ml_conv_b", "ml_wq", "ml_wk", "ml_wv", "ml_bi", "ml_bf", "ml_norm_g", "w_out",
        "xa_norm_g", "mem_norm_g", "xa_wq", "xa_wkv", "xa_wo", "final_norm_g", "mem_2", "g_pre_2", "g_post_2",
        "g_mem_2", "w_in_2", "b_merge_2", "w_pool_2", "pool_scale_2", "w_alpha_2", "b_alpha_2", "g_gla_2",
        "w_mem_kv_2", "w_br_pool_2", "w_br_swa_2", "w_br_gla_2", "w_br_mem_2", "w_out_2"]


def kernel(**inputs):
    import numpy as _np
    import concourse.bacc as _bacc
    from concourse import mybir as _mybir
    from concourse.bass_utils import run_bass_kernel_spmd as _run

    nc = _bacc.Bacc("TRN2", target_bir_lowering=False, num_devices=1)
    arrays, args = {}, {}
    for name in _INS:
        x = _np.ascontiguousarray(inputs[name])
        arrays[f"in_{name}_dram"] = x
        args[name] = nc.dram_tensor(f"in_{name}_dram", x.shape, _mybir.dt.from_np(x.dtype), kind="ExternalInput").ap()
    out = nc.dram_tensor("out_0_dram", (1, T, D), F32, kind="ExternalOutput").ap()
    build(nc, args, out)
    r = _run(nc, [arrays], core_ids=[0])
    return r.results[0]["out_0_dram"]
```
